# Optimizing a Trainium2 kernel written in Bass

```python
import math
import jax, jax.numpy as jnp
from jax import lax
import numpy as np

D_MODEL = 1024
BATCH = 1
SEQ = 512
DEPTH = 1

CHUNK = 64
ATT_HEADS = 16
ATT_KV_HEADS = 2
ATT_HEAD_DIM = 64
ATT_GROUP = ATT_HEADS // ATT_KV_HEADS
WINDOW = 128
WINDOW_CHUNKS = WINDOW // CHUNK
ATT_Q_W = ATT_HEADS * ATT_HEAD_DIM
ATT_KV_W = ATT_KV_HEADS * ATT_HEAD_DIM
DN_HEADS = 8
DN_KEY_DIM = 128
DN_VAL_DIM = 128
DN_QK_W = DN_HEADS * DN_KEY_DIM
DN_V_W = DN_HEADS * DN_VAL_DIM
CONV_K = 4
CONV_W = 2 * DN_QK_W + DN_V_W
N_BRANCHES = 2
IN_SPLITS = (ATT_Q_W, ATT_KV_W, ATT_KV_W, CONV_W, DN_HEADS, DN_HEADS, DN_V_W, N_BRANCHES * D_MODEL)
IN_COLS = sum(IN_SPLITS)
D_FF = 4 * D_MODEL
EPS = 1e-6
NEG_BIG = -1e30

kernel_name = "hybrid_swa_sink_gated_deltanet_block"

def _split_cols(z, sizes):
    out, start = [], 0
    for s in sizes:
        out.append(z[..., start:start + s])
        start += s
    return out

def rms_norm(x, w):
    xf = x.astype(jnp.float32)
    y = xf * lax.rsqrt(jnp.mean(xf * xf, axis=-1, keepdims=True) + EPS)
    return (y * w.astype(jnp.float32)).astype(x.dtype)

def l2_normalize(x):
    xf = x.astype(jnp.float32)
    return xf * lax.rsqrt(jnp.sum(xf * xf, axis=-1, keepdims=True) + EPS)

def sliding_window_sink_attention(q, k, v, sinks):
    B, S, _ = q.shape
    nc = S // CHUNK
    span = WINDOW_CHUNKS * CHUNK
    q = q.reshape(B, nc, CHUNK, ATT_KV_HEADS, ATT_GROUP, ATT_HEAD_DIM)
    k = k.reshape(B, nc, CHUNK, ATT_KV_HEADS, ATT_HEAD_DIM)
    v = v.reshape(B, nc, CHUNK, ATT_KV_HEADS, ATT_HEAD_DIM)

    def band(t):
        padded = jnp.pad(t, ((0, 0), (WINDOW_CHUNKS - 1, 0), (0, 0), (0, 0), (0, 0)))
        return jnp.concatenate([padded[:, w:w + nc] for w in range(WINDOW_CHUNKS)], axis=2)

    kb, vb = band(k), band(v)
    scores = jnp.einsum('bncjgd,bnmjd->bnjgcm', q, kb,
                        preferred_element_type=jnp.float32) * (ATT_HEAD_DIM ** -0.5)
    key_chunk = (jnp.arange(nc)[:, None] - (WINDOW_CHUNKS - 1)
                 + jnp.arange(span)[None, :] // CHUNK)
    valid = (key_chunk >= 0)[None, :, None, None, None, :]
    scores = jnp.where(valid, scores, NEG_BIG)
    sink = sinks.astype(jnp.float32).reshape(ATT_KV_HEADS, ATT_GROUP)[None, None, :, :, None, None]
    lse = jnp.logaddexp(jax.nn.logsumexp(scores, axis=-1, keepdims=True), sink)
    probs = jnp.exp(scores - lse)
    out = jnp.einsum('bnjgcm,bnmjd->bncjgd', probs.astype(vb.dtype), vb)
    return out.reshape(B, S, ATT_Q_W)

def causal_short_conv(x, w):
    S = x.shape[1]
    xp = jnp.pad(x, ((0, 0), (CONV_K - 1, 0), (0, 0)))
    y = xp[:, 0:S] * w[0]
    for i in range(1, CONV_K):
        y = y + xp[:, i:i + S] * w[i]
    return y

def gated_delta_rule(q, k, v, g, beta):
    B, S, H, dk = q.shape
    dv = v.shape[-1]
    nc = S // CHUNK
    q = q * (dk ** -0.5)

    def chunks4(t):
        return t.reshape(B, nc, CHUNK, H, t.shape[-1]).transpose(0, 1, 3, 2, 4)

    def chunks3(t):
        return t.reshape(B, nc, CHUNK, H).transpose(0, 1, 3, 2)

    qc, kc, vc = chunks4(q), chunks4(k), chunks4(v)
    bc = chunks3(beta)
    G = jnp.cumsum(chunks3(g), axis=-1)
    causal = jnp.tril(jnp.ones((CHUNK, CHUNK), dtype=bool))
    strict = jnp.tril(jnp.ones((CHUNK, CHUNK), dtype=bool), k=-1)
    decay = jnp.exp(jnp.where(causal, G[..., :, None] - G[..., None, :], -jnp.inf))
    kk = jnp.einsum('bnhcd,bnhmd->bnhcm', kc, kc)
    L = jnp.where(strict, bc[..., None] * kk * decay, 0.0)
    rhs = jnp.concatenate([vc * bc[..., None], kc * (bc * jnp.exp(G))[..., None]], axis=-1)
    sol = lax.linalg.triangular_solve(L, rhs, left_side=True, lower=True, unit_diagonal=True)
    U, W = sol[..., :dv], sol[..., dv:]
    intra = jnp.einsum('bnhcd,bnhmd->bnhcm', qc, kc) * decay
    q_dec = qc * jnp.exp(G)[..., None]
    k_dec = kc * jnp.exp(G[..., -1:] - G)[..., None]
    g_last = jnp.exp(G[..., -1])

    def step(state, inp):
        qd, kd, u, w, a, gl = inp
        v_new = u - jnp.einsum('bhcd,bhde->bhce', w, state)
        o = jnp.einsum('bhcd,bhde->bhce', qd, state) + jnp.einsum('bhcm,bhme->bhce', a, v_new)
        state = state * gl[..., None, None] + jnp.einsum('bhcd,bhce->bhde', kd, v_new)
        return state, o

    xs = tuple(jnp.moveaxis(t, 1, 0) for t in (q_dec, k_dec, U, W, intra, g_last))
    state0 = jnp.zeros((B, H, dk, dv), jnp.float32)
    _, o = lax.scan(step, state0, xs)
    return o.transpose(1, 0, 3, 2, 4).reshape(B, S, H, dv)

def hybrid_mixer(h, w_in, b_gate, attn_sinks, conv_w, a_log, dt_bias, dn_norm_w,
                 w_branch_attn, w_branch_delta, w_out):
    B, S, _ = h.shape
    z = h @ w_in
    aq, ak, av, dqkv, db, da, dz, gate_logits = _split_cols(z, IN_SPLITS)

    y_att = sliding_window_sink_attention(aq, ak, av, attn_sinks)

    dqkv = jax.nn.silu(causal_short_conv(dqkv, conv_w))
    dq, dk, dv = _split_cols(dqkv, (DN_QK_W, DN_QK_W, DN_V_W))
    dq = l2_normalize(dq.reshape(B, S, DN_HEADS, DN_KEY_DIM))
    dk = l2_normalize(dk.reshape(B, S, DN_HEADS, DN_KEY_DIM))
    dv = dv.reshape(B, S, DN_HEADS, DN_VAL_DIM).astype(jnp.float32)
    beta = jax.nn.sigmoid(db.astype(jnp.float32))
    g = -jnp.exp(a_log.astype(jnp.float32)) * jax.nn.softplus(
        da.astype(jnp.float32) + dt_bias.astype(jnp.float32))
    o = gated_delta_rule(dq, dk, dv, g, beta)
    o = o * lax.rsqrt(jnp.mean(o * o, axis=-1, keepdims=True) + EPS)
    o = o * dn_norm_w.astype(jnp.float32) * jax.nn.silu(
        dz.reshape(B, S, DN_HEADS, DN_VAL_DIM).astype(jnp.float32))
    y_dn = o.reshape(B, S, DN_V_W).astype(h.dtype)

    gates = jax.nn.sigmoid(gate_logits + b_gate)
    g_att, g_dn = gates[..., :D_MODEL], gates[..., D_MODEL:]
    merged = g_att * (y_att @ w_branch_attn) + g_dn * (y_dn @ w_branch_delta)
    return merged @ w_out

def setup_inputs(seed: int = 0) -> dict:
    key = jax.random.key(seed)
    ks = jax.random.split(key, 16)
    f32 = jnp.float32

    def normal(k, shape, scale):
        return jax.random.normal(k, shape, f32) * scale

    x = normal(ks[0], (BATCH, SEQ, D_MODEL), 1.0)
    norm_mix_w = 1.0 + normal(ks[1], (DEPTH, D_MODEL), 0.02)
    w_in = normal(ks[2], (DEPTH, D_MODEL, IN_COLS), D_MODEL ** -0.5)
    b_gate = normal(ks[3], (DEPTH, N_BRANCHES * D_MODEL), 0.02)
    attn_sinks = normal(ks[4], (DEPTH, ATT_HEADS), 0.5)
    conv_w = normal(ks[5], (DEPTH, CONV_K, CONV_W), CONV_K ** -0.5)
    a_log = jnp.log(jax.random.uniform(ks[6], (DEPTH, DN_HEADS), f32, 1.0, 16.0))
    dt = jnp.exp(jax.random.uniform(ks[7], (DEPTH, DN_HEADS), f32, math.log(1e-3), math.log(1e-1)))
    dt_bias = dt + jnp.log(-jnp.expm1(-dt))
    dn_norm_w = 1.0 + normal(ks[8], (DEPTH, DN_VAL_DIM), 0.02)
    w_branch_attn = normal(ks[9], (DEPTH, ATT_Q_W, D_MODEL), ATT_Q_W ** -0.5)
    w_branch_delta = normal(ks[10], (DEPTH, DN_V_W, D_MODEL), DN_V_W ** -0.5)
    w_out = normal(ks[11], (DEPTH, D_MODEL, D_MODEL), D_MODEL ** -0.5)
    norm_mlp_w = 1.0 + normal(ks[12], (DEPTH, D_MODEL), 0.02)
    w_mlp_up = normal(ks[13], (DEPTH, D_MODEL, D_FF), D_MODEL ** -0.5)
    w_mlp_down = normal(ks[14], (DEPTH, D_FF, D_MODEL), 0.5 * D_FF ** -0.5)
    final_norm_w = 1.0 + normal(ks[15], (D_MODEL,), 0.02)
    return {"x": x, "norm_mix_w": norm_mix_w, "w_in": w_in, "b_gate": b_gate,
            "attn_sinks": attn_sinks, "conv_w": conv_w, "a_log": a_log, "dt_bias": dt_bias,
            "dn_norm_w": dn_norm_w, "w_branch_attn": w_branch_attn,
            "w_branch_delta": w_branch_delta, "w_out": w_out, "norm_mlp_w": norm_mlp_w,
            "w_mlp_up": w_mlp_up, "w_mlp_down": w_mlp_down, "final_norm_w": final_norm_w}

def reference(x, norm_mix_w, w_in, b_gate, attn_sinks, conv_w, a_log, dt_bias, dn_norm_w,
              w_branch_attn, w_branch_delta, w_out, norm_mlp_w, w_mlp_up, w_mlp_down,
              final_norm_w):
    for l in range(DEPTH):
        h = rms_norm(x, norm_mix_w[l])
        x = x + hybrid_mixer(h, w_in[l], b_gate[l], attn_sinks[l], conv_w[l], a_log[l],
                             dt_bias[l], dn_norm_w[l], w_branch_attn[l], w_branch_delta[l],
                             w_out[l])
        h = rms_norm(x, norm_mlp_w[l])
        x = x + jnp.square(jax.nn.relu(h @ w_mlp_up[l])) @ w_mlp_down[l]
    return rms_norm(x, final_norm_w)


_drawn_inputs = setup_inputs


def setup_inputs(seed=0):
    import zlib

    import numpy as np

    out = dict(_drawn_inputs(seed))
    spreads = {}
    factors = {'norm_mix_w': 4.726,
     'b_gate': 8.0,
     'attn_sinks': 8.0,
     'dn_norm_w': 8.0,
     'norm_mlp_w': 18.808,
     'final_norm_w': 8.08}
    for name, (base, spread) in spreads.items():
        noise = np.random.default_rng([zlib.crc32(name.encode()), seed]).standard_normal(out[name].shape)
        drawn = base * np.exp(spread * noise) if base else spread * noise
        out[name] = __import__('jax').numpy.asarray(drawn.astype(out[name].dtype))
    for name, factor in factors.items():
        out[name] = (out[name] * factor).astype(out[name].dtype)
    return out
```

```python
import math
from contextlib import ExitStack

import concourse.bass as bass
from concourse import mybir
from concourse.alu_op_type import AluOpType as ALU

F32 = mybir.dt.float32
F32R = mybir.dt.float32r
ACT = mybir.ActivationFunctionType
AX_X = mybir.AxisListType.X

P = 128
D = 1024
S = 512
KT = D // P
TT = S // P
C = 64
HD = 64
NH = 8
FF = 4096
EPS = 1e-6
LN_Q_SCALE = -0.5 * math.log(128)
NEG = -1e30
HALVES = 2
GH = NH // HALVES

COL_Q, COL_K, COL_V, COL_CONV = 0, 1024, 1152, 1280
COL_BETA = COL_CONV + 3 * D
COL_DZ = COL_BETA + 2 * NH
COL_GATE = COL_DZ + D

N_CONV, N_DN, N_KV, N_GATE, N_BR, N_OUT, N_UP, N_DOWN = 24, 16, 2, 16, 8, 8, 32, 32
B_CONV = 0
B_DN = B_CONV + N_CONV
B_KV = B_DN + N_DN
B_GATE = B_KV + N_KV
B_BRA = B_GATE + N_GATE
B_BRD = B_BRA + N_BR
B_OUT = B_BRD + N_BR
B_UP = B_OUT + N_OUT
B_DOWN = B_UP + N_UP
B_END = B_DOWN + N_DOWN
WS = 4
RS = 2

PR_CONV, PR_MIX, PR_GATE, PR_MLP = 0, 96, 104, 120

CONSTS = ["ident", "ones", "tri", "later", "mask_t", "mask_l", "m1", "m1t", "m2", "m4", "m8", "m16", "m32"]
LEVELS = ["m2", "m4", "m8", "m16", "m32"]

QKV = 0
YD = 24 * S
W0 = YD + 8 * S
(O_KQ, O_KD, O_X, O_T, O_Y, O_LT, O_INT, O_L, O_VTOK, O_R, O_VN, O_S, O_O, O_END) = (
    W0 + 1024 * k for k in (0, 2, 4, 5, 6, 7, 8, 9, 10, 11, 12, 13, 14, 15))
O_GATES = W0
O_P, O_PT, O_QS = W0 + 8192, W0 + 9216, W0 + 10240
O_KVS, O_KVT, O_VT2 = W0 + 11264, W0 + 12032, W0 + 13760
O_YATT = QKV + 16 * S
O_XN, O_PROW, O_JUNK0 = W0, W0 + 5120, W0 + 6144
O_X1, O_FW, O_JUNK1 = W0 + 8192, W0 + 12288, W0 + 4096
O_CONST = O_END
O_PT_PAR = O_CONST + 128 * len(CONSTS)
O_SMALL = O_PT_PAR + 128
ARENA = O_SMALL + 512


def build(nc, x, norm_mix_w, w_in, b_gate, attn_sinks, conv_w, a_log, dt_bias, dn_norm_w,
          w_branch_attn, w_branch_delta, w_out, norm_mlp_w, w_mlp_up, w_mlp_down, final_norm_w,
          shape_consts, out):
    w_in_v = w_in[0].rearrange("(k p) n -> p k n", p=P)
    bra_v = w_branch_attn[0].rearrange("(k p) n -> p k n", p=P)
    brd_v = w_branch_delta[0].rearrange("(k p) n -> p k n", p=P)
    up_v = w_mlp_up[0].rearrange("(k p) n -> p k n", p=P)
    x_v = x[0].rearrange("(t p) n -> p t n", p=P)
    out_v = out[0].rearrange("(t p) n -> p t n", p=P)

    with ExitStack() as ctx:
        def sem(name):
            return ctx.enter_context(nc.semaphore(name))

        arena = ctx.enter_context(nc.sbuf_tensor("arena", [P, ARENA], F32))
        raw = ctx.enter_context(nc.sbuf_tensor("raw", [P, RS, D], F32))
        w_hi = ctx.enter_context(nc.sbuf_tensor("w_hi", [P, WS, D], F32R))
        w_lo = ctx.enter_context(nc.sbuf_tensor("w_lo", [P, WS, D], F32R))
        act_hi = ctx.enter_context(nc.sbuf_tensor("act_hi", [P, KT, S], F32R))
        act_lo = ctx.enter_context(nc.sbuf_tensor("act_lo", [P, KT, S], F32R))
        wb_hi = ctx.enter_context(nc.sbuf_tensor("wb_hi", [P, KT * 2 * NH], F32R))
        wb_lo = ctx.enter_context(nc.sbuf_tensor("wb_lo", [P, KT * 2 * NH], F32R))
        ps = ctx.enter_context(nc.psum_tensor("ps", [P, 8, 512], F32))

        def flat(off, n, p0=0, p1=P):
            return arena[p0:p1, off:off + n]

        def grid(off, a, b):
            return arena[:, off:off + a * b].rearrange("p (a b) -> p a b", a=a)

        def heads(bank):
            return ps[:, bank:bank + 2, :].rearrange("p b (h n) -> p (b h) n", n=128)

        qkv = grid(QKV, 24, S)
        yd = grid(YD, NH, S)
        KQ = arena[:, O_KQ:O_KQ + 2048].rearrange("p (h s n) -> p h s n", h=NH, s=2)
        KD = arena[:, O_KD:O_KD + 2048].rearrange("p (h c s n) -> p h c s n", h=NH, c=2, s=2)
        X, T, Y, LT, INT, L, VTOK, R, VN, ST, O = (
            grid(o, NH, 128) for o in (O_X, O_T, O_Y, O_LT, O_INT, O_L, O_VTOK, O_R, O_VN, O_S, O_O))
        EG, VS, TAILK = R, VN, L
        gates = grid(O_GATES, 16, S)
        PR, PT = grid(O_P, 8, 128), grid(O_PT, 8, 128)
        qs = [grid(O_QS + 512 * c, 8, C) for c in range(2)]
        kvs = [grid(O_KVS + 384 * c, 3, 128) for c in range(2)]
        kvt = grid(O_KVT, 3, S + C)
        vt2 = [flat(O_VT2 + 128 * c, 128) for c in range(2)]
        yatt = grid(O_YATT, KT, S)
        xn = grid(O_XN, TT, D)
        x1 = grid(O_X1, TT, D)
        fw = flat(O_FW, D)
        a_t = grid(0, N_UP, S)
        const = {n: flat(O_CONST + 128 * i, 128) for i, n in enumerate(CONSTS)}
        par = flat(O_PT_PAR, 128)

        at = [O_SMALL]

        def small(n):
            at[0] += n
            assert at[0] <= ARENA
            return flat(at[0] - n, n)

        ss, rstd = small(4), small(4)
        beta, dec, gcol, tail = small(32), small(32), small(32), small(32)
        alog, dtb = small(8), small(8)
        sinks, sinks_all = small(8), small(16)
        dnw = small(1)
        wbeta = small(KT * 2 * NH)
        g_now = small(8)
        gl = small(16)
        oss, ors = small(8), small(8)
        mx, es, den = small(8), small(8), small(8)
        tmp = [small(32), small(32)]
        eps_c, lnq_c, zero_c = small(1), small(1), small(1)
        beta3, dec3, gcol3, tail3 = (a.rearrange("p (t h) -> p t h", h=NH) for a in (beta, dec, gcol, tail))
        gl3 = gl.rearrange("p (h c) -> p h c", c=2)
        bd_cols = ps[:, 3, 0:TT * 2 * NH].rearrange("p (t n) -> p t n", t=TT)
        prow = flat(O_PROW, 128)
        bd_rows = arena[0:2 * NH, YD:YD + S]

        def mat(name, n=NH):
            return const[name].unsqueeze(1).to_broadcast([P, n, 128])

        def col(a, n=NH):
            return a.unsqueeze(2).to_broadcast([a.shape[0], n, 128])

        consts_in, x_in, params_in, small_in, wb_in, x_again, out_sent = map(
            sem, ["consts_in", "x_in", "params_in", "small_in", "wb_in", "x_again", "out_sent"])
        raw_in = [sem(f"raw_in{i}") for i in range(RS)]
        w_hi_ok, w_ok, blk_mm, blk_read = map(sem, ["w_hi_ok", "w_ok", "blk_mm", "blk_read"])
        a_hi_ok, a_ok = sem("a_hi_ok"), sem("a_ok")
        par_mm, par_ok, ss_ok, ln_ok, rstd_ok, xn_ok, xt_mm = map(
            sem, ["par_mm", "par_ok", "ss_ok", "ln_ok", "rstd_ok", "xn_ok", "xt_mm"])
        wb_hi_ok, wb_ok, bd_mm, bd_ok, bdt_mm, sm, sm_act, g_ok, gc_mm, gc_ok, gt_ok = map(
            sem, ["wb_hi_ok", "wb_ok", "bd_mm", "bd_ok", "bdt_mm", "sm", "sm_act", "g_ok", "gc_mm", "gc_ok", "gt_ok"])
        conv_tap, conv_ok, eps_ok, sink_ok = sem("conv_tap"), sem("conv_ok"), sem("eps_ok"), sem("sink_ok")
        (sq_ok, ss_mm, lns_ok, rn_ok, g_now_ok, grow_mm, eg_ok, gl_ok, kq_ok, arg_ok, darg_ok, dexp_ok, gram_mm,
         l_raw, l_ok, int_ok, vs_ok, lt_mm, vt_mm, kt_mm, lt_ok, vtok_ok, y1_ok, x0_ok, y2_ok, t0_ok, kdec_ok,
         y_mm, y_ok, xt2_mm, x_upd, t_upd, tb_ok, kdq_ok, kq_mm, r_ok, vn_mm, vn_ok, o_mm, su_mm, s_upd, o_ok,
         osq_ok, oss_ok, oln_ok, ors_ok, on_ok, on_mm, yd_ok, s0_ok) = map(sem, [
            "sq_ok", "ss_mm", "lns_ok", "rn_ok", "g_now_ok", "grow_mm", "eg_ok", "gl_ok", "kq_ok", "arg_ok",
            "darg_ok", "dexp_ok", "gram_mm", "l_raw", "l_ok", "int_ok", "vs_ok", "lt_mm", "vt_mm", "kt_mm",
            "lt_ok", "vtok_ok", "y1_ok", "x0_ok", "y2_ok", "t0_ok", "kdec_ok", "y_mm", "y_ok", "xt2_mm",
            "x_upd", "t_upd", "tb_ok", "kdq_ok", "kq_mm", "r_ok", "vn_mm", "vn_ok", "o_mm", "su_mm", "s_upd",
            "o_ok", "osq_ok", "oss_ok", "oln_ok", "ors_ok", "on_ok", "on_mm", "yd_ok", "s0_ok"])
        (dz_ok, ydz_ok, kv_pad, kv_ok, qs_ok, kvs_ok, sc_mm, vw_mm, vw_ok, mx_ok, m_ok, pe_ok, esd_ok, exp_ok,
         es_ok, den_ok, rden_ok, pn_ok, pt_mm, pt_ok, pv_mm, ya_ok) = map(sem, [
            "dz_ok", "ydz_ok", "kv_pad", "kv_ok", "qs_ok", "kvs_ok", "sc_mm", "vw_mm", "vw_ok", "mx_ok", "m_ok",
            "pe_ok", "esd_ok", "exp_ok", "es_ok", "den_ok", "rden_ok", "pn_ok", "pt_mm", "pt_ok", "pv_mm", "ya_ok"])
        sig_ok, relu_ok, mg_ok, x1_ok, y_add, y_fin, fw_ok = map(
            sem, ["sig_ok", "relu_ok", "mg_ok", "x1_ok", "y_add", "y_fin", "fw_ok"])

        apart_sem = sem("apart")

        def apart(engine):
            engine.sem_inc(apart_sem, 1)

        block = ctx.enter_context(nc.Block())

        @block.sync
        def _(sp):
            def load(b, i, src):
                if b >= RS:
                    sp.wait_ge(w_ok, b + WS * i - RS + 1)
                    if not isinstance(i, int):
                        apart(sp)
                dst = raw[:, b % RS, :]
                if len(src.shape) == 3:
                    dst = dst.rearrange("p (k n) -> p k n", k=KT)
                sp.dma_start(dst, src).then_inc(raw_in[b % RS], 16)

            def cols(view, c):
                return view[:, :, bass.ds(c, 128)]

            for t in range(TT):
                sp.dma_start(xn[:, t, :], x_v[:, t, :]).then_inc(x_in, 16)
            sp.dma_start(prow[PR_CONV:PR_MIX, :], conv_w[0].rearrange("t (b p) -> (t b) p", p=P)).then_inc(params_in, 16)
            sp.dma_start(prow[PR_MIX:PR_GATE, :], norm_mix_w[0].rearrange("(b p) -> b p", p=P)).then_inc(params_in, 16)
            sp.dma_start(prow[PR_GATE:PR_MLP, :], b_gate[0].rearrange("(b p) -> b p", p=P)).then_inc(params_in, 16)
            sp.dma_start(prow[PR_MLP:P, :], norm_mlp_w[0].rearrange("(b p) -> b p", p=P)).then_inc(params_in, 16)
            cflat = arena[:, O_CONST:O_CONST + 128 * len(CONSTS)]
            sp.dma_start(cflat, shape_consts.rearrange("p a b -> p (a b)")).then_inc(consts_in, 16)
            sp.dma_start(wbeta.rearrange("p (k n) -> p k n", k=KT),
                         w_in_v[:, :, COL_BETA:COL_BETA + 2 * NH]).then_inc(wb_in, 16)
            load(0, 0, cols(w_in_v, COL_CONV))
            load(1, 0, cols(w_in_v, COL_CONV + 128))
            sp.dma_start(alog, a_log[0:1, :].to_broadcast([P, NH])).then_inc(small_in, 16)
            sp.dma_start(dtb, dt_bias[0:1, :].to_broadcast([P, NH])).then_inc(small_in, 16)
            sp.dma_start(dnw, dn_norm_w.rearrange("a p -> p a")).then_inc(small_in, 16)
            sp.dma_start(sinks_all, attn_sinks[0:1, :].to_broadcast([P, 16])).then_inc(small_in, 16)
            for b in range(2, WS):
                load(b, 0, cols(w_in_v, COL_CONV + 128 * b))
            with sp.Fori(0, N_CONV // WS - 1) as i:
                for k in range(WS):
                    load(WS + k, i, cols(w_in_v, i * 512 + (COL_CONV + 512 + 128 * k)))
            with sp.Fori(0, TT) as t:
                for k, c in enumerate((COL_DZ, COL_DZ + 128, COL_Q, COL_Q + 128)):
                    load(B_DN + k, t, cols(w_in_v, t * 256 + c))
            load(B_KV, 0, cols(w_in_v, COL_K))
            load(B_KV + 1, 0, cols(w_in_v, COL_V))
            with sp.Fori(0, N_GATE // WS) as i:
                for k in range(WS):
                    load(B_GATE + k, i, cols(w_in_v, i * 512 + (COL_GATE + 128 * k)))
            for b0, view in ((B_BRA, bra_v), (B_BRD, brd_v)):
                with sp.Fori(0, N_BR // WS) as i:
                    for k in range(WS):
                        load(b0 + k, i, cols(view, i * 512 + 128 * k))
            sp.wait_ge(ya_ok, S // C)
            sp.dma_start(x1[:, :, :], x_v[:, :, :]).then_inc(x_again, 16)
            with sp.Fori(0, N_OUT // WS) as i:
                for k in range(WS):
                    load(B_OUT + k, i, w_out[0, bass.ds(i * 512 + 128 * k, 128), :])
            sp.dma_start(fw, final_norm_w.unsqueeze(0).to_broadcast([P, D])).then_inc(fw_ok, 16)
            with sp.Fori(0, N_UP // WS) as i:
                for k in range(WS):
                    load(B_UP + k, i, cols(up_v, i * 512 + 128 * k))
            with sp.Fori(0, N_DOWN // WS) as i:
                for k in range(WS):
                    load(B_DOWN + k, i, w_mlp_down[0, bass.ds(i * 512 + 128 * k, 128), :])
            for t in range(TT):
                sp.wait_ge(y_fin, t + 1)
                sp.dma_start(out_v[:, t, :], x1[:, t, :]).then_inc(out_sent, 16)
            sp.wait_ge(out_sent, 16 * TT)

        @block.gpsimd
        def _(pool):
            def lo(b, i=0):
                pool.wait_ge(w_hi_ok, b + WS * i + 1)
                pool.tensor_tensor(w_lo[:, b % WS, :], raw[:, b % RS, :], w_hi[:, b % WS, :].bitcast(F32),
                                   ALU.subtract).then_inc(w_ok, 1)

            with pool.Fori(0, N_CONV // WS + 1) as i:
                for k in range(WS):
                    lo(k, i)
            with pool.Fori(0, TT) as t:
                pool.wait_ge(kq_ok, t * 2 + 2)
                pool.wait_ge(eg_ok, t + 1)
                for c in range(2):
                    for s, part in ((0, c), (1, 1 - c)):
                        pool.tensor_tensor(KD[:, :, c, part, :], KQ[:, :, s, C * c:C * c + C],
                                           EG[:, :, C * c:C * c + C], ALU.mult).then_inc(kdq_ok, 1)
                for k in range(WS):
                    lo(B_DN + WS + k, t)
            lo(B_KV + WS)
            lo(B_KV + WS + 1)
            with pool.Fori(0, S // P) as s:
                for c in range(2):
                    pool.wait_ge(rden_ok, s * 2 + (c + 1))
                    pool.tensor_tensor(PR, PR, col(den), ALU.mult).then_inc(pn_ok, 1)
                    lo(B_GATE + WS + 2 * c, s)
                    lo(B_GATE + WS + 2 * c + 1, s)
            with pool.Fori(0, (B_END - B_BRA) // WS - 1) as i:
                for k in range(WS):
                    lo(B_BRA + WS + k, i)

        @block.tensor
        def _(pe):
            def products(out_ap, lhs, rhs, first, last):
                m = None
                for n, (a, b) in enumerate(((0, 0), (0, 1), (1, 0))):
                    m = pe.matmul(out_ap, lhs[a], rhs[b], start=first and n == 0, stop=last and n == 2)
                return m

            def block_f(b, i=0, tiles=None):
                pe.wait_ge(w_ok, b + WS * i + 1)
                f = b if b < B_OUT else b - N_OUT
                if f >= 2:
                    pe.wait_ge(blk_read, f + WS * i - 1)
                for k in range(KT):
                    w = [h[:, b % WS, 128 * k:128 * k + 128] for h in (w_hi, w_lo)]
                    if tiles is not None:
                        pe.wait_ge(a_ok, tiles + k + 1)
                    m = products(ps[:, f % 2, :], w, (act_hi[:, k, :], act_lo[:, k, :]), k == 0, k == KT - 1)
                m.then_inc(blk_mm, 1)

            def block_t(b, i, slot, first, last):
                pe.wait_ge(w_ok, b + WS * i + 1)
                for t in range(TT):
                    a = [h[:, slot, 128 * t:128 * t + 128] for h in (act_hi, act_lo)]
                    for n in range(2):
                        w = [h[:, b % WS, 512 * n:512 * n + 512] for h in (w_hi, w_lo)]
                        m = products(ps[:, 2 * t + n, :], a, w, first, last)
                m.then_inc(blk_mm, 1)

            def transposes_in(tiles):
                for t in range(TT):
                    pe.wait_ge(xn_ok, tiles + t + 1)
                    for k in range(KT):
                        m = pe.transpose(ps[:, k, 128 * t:128 * t + 128], xn[:, t, 128 * k:128 * k + 128], const["ident"])
                m.then_inc(xt_mm, 1)

            pe.wait_ge(consts_in, 16)
            pe.wait_ge(params_in, 4 * 16)
            pe.transpose(ps[:, 0, 0:128], prow, const["ident"]).then_inc(par_mm, 1)
            pe.wait_ge(par_ok, 1)
            transposes_in(0)
            pe.wait_ge(wb_ok, 1)
            pe.wait_ge(a_ok, KT)
            for k in range(KT):
                w = [wb[:, 2 * NH * k:2 * NH * (k + 1)] for wb in (wb_hi, wb_lo)]
                m = products(ps[0:2 * NH, 2, :], w, (act_hi[:, k, :], act_lo[:, k, :]), k == 0, k == KT - 1)
            m.then_inc(bd_mm, 1)
            block_f(0)
            pe.wait_ge(bd_ok, 1)
            for t in range(TT):
                m = pe.transpose(ps[:, 3, 16 * t:16 * t + 16], bd_rows[:, 128 * t:128 * t + 128], const["ident"][0:16, 0:16])
            m.then_inc(bdt_mm, 1)
            for b in range(1, WS):
                block_f(b)
            with pe.Fori(0, N_CONV // WS - 1) as i:
                for k in range(WS):
                    block_f(WS + k, i)
            pe.wait_ge(g_ok, 1)
            pe.matmul(ps[:, 3, 0:32], const["tri"], dec, start=True, stop=True)
            pe.matmul(ps[:, 4, 0:32], const["later"], dec, start=True, stop=True).then_inc(gc_mm, 1)
            pe.wait_ge(gc_ok, 2)
            pe.wait_ge(s0_ok, 1)

            with pe.Fori(0, TT) as t:
                for n in range(2):
                    pe.wait_ge(sq_ok, t * 2 + (n + 1))
                    for g in range(HALVES):
                        m = pe.matmul(ps[:, 2 + 2 * n + g, :], const["ones"],
                                      (X, T)[n][:, GH * g:GH * g + GH, :], start=True, stop=True)
                    m.then_inc(ss_mm, 1)
                pe.wait_ge(g_now_ok, t + 1)
                for h in range(NH):
                    m = pe.matmul(heads(6)[:, h, :], g_now[:, h:h + 1].to_broadcast([P, 128]), const["tri"],
                                  start=h % GH == 0, stop=True, skip_group_check=True)
                m.then_inc(grow_mm, 1)
                block_f(B_DN, t)
                pe.wait_ge(kq_ok, t * 2 + 2)
                pe.wait_ge(lns_ok, t * 2 + 2)
                for h in range(NH):
                    m = pe.matmul(ps[:, 2 + h // 2, 256 * (h % 2):256 * (h % 2) + 256], KQ[:, h, 0, :],
                                  KQ[:, h, :, :], start=h % 2 == 0, stop=True, skip_group_check=True)
                m.then_inc(gram_mm, 1)
                block_f(B_DN + 1, t)
                pe.wait_ge(vs_ok, t + 1)
                pe.wait_ge(l_raw, t + 1)
                pe.wait_ge(int_ok, t + 1)
                for h in range(NH):
                    m = pe.transpose(heads(2)[:, h, :], VS[:, h, :], const["ident"])
                m.then_inc(vt_mm, 1)
                for h in range(NH):
                    m = pe.transpose(heads(4)[:, h, :], KQ[:, h, 0, :], const["ident"])
                m.then_inc(kt_mm, 1)
                pe.wait_ge(l_ok, t + 1)
                pe.wait_ge(eg_ok, t + 1)
                for h in range(NH):
                    m = pe.transpose(heads(6)[:, h, :], L[:, h, :], const["ident"])
                m.then_inc(lt_mm, 1)
                for lv in range(len(LEVELS)):
                    last = lv == len(LEVELS) - 1
                    for g in range(HALVES):
                        if lv == 0:
                            pe.wait_ge(lt_ok, t + 1)
                            pe.wait_ge(x0_ok, t + 1)
                            pe.wait_ge(vtok_ok, t + 1)
                        else:
                            pe.wait_ge(x_upd, t * 8 + (2 * lv - 1 + g))
                        for h in range(GH * g, GH * g + GH):
                            m = pe.matmul(heads(2)[:, h, :], LT[:, h, :], X[:, h, :], start=h % GH == 0, stop=True,
                                          skip_group_check=True)
                        m.then_inc(y_mm, 1)
                    for g in range(HALVES):
                        pe.wait_ge(y_ok, t * 10 + (2 * lv + g + 1))
                        if lv == 0:
                            pe.wait_ge(t0_ok, t + 1)
                            pe.wait_ge(kdec_ok, t + 1)
                        else:
                            pe.wait_ge(t_upd, t * 10 + (2 * lv - 1 + g))
                        if not last:
                            for h in range(GH * g, GH * g + GH):
                                pe.matmul(heads(4)[:, h, :], T[:, h, :], Y[:, h, :], start=h % GH == 0, stop=True,
                                          skip_group_check=True)
                        for h in range(GH * g, GH * g + GH):
                            m = pe.matmul(heads(6)[:, h, :], Y[:, h, :], T[:, h, :], start=h % GH == 0, stop=True,
                                          skip_group_check=True)
                        m.then_inc(xt2_mm, 1)
                block_f(B_DN + 2, t)
                pe.wait_ge(tb_ok, t + 1)
                pe.wait_ge(kdq_ok, t * 4 + 4)
                for c in range(2):
                    p0 = C * c
                    own, other = slice(p0, p0 + C), slice(C - p0, 2 * C - p0)
                    for g in range(HALVES):
                        if c:
                            pe.wait_ge(s_upd, t * 4 + (1 + g))
                            pe.wait_ge(o_ok, t * 4 + (1 + g))
                        for h in range(GH * g, GH * g + GH):
                            m = pe.matmul(heads(2)[:, h, :], KD[:, h, c, :, :].rearrange("p s n -> p (s n)"), ST[:, h, :],
                                          start=h % GH == 0, stop=False, skip_group_check=True)
                        m.then_inc(kq_mm, 1)
                    for g in range(HALVES):
                        pe.wait_ge(r_ok, t * 4 + (2 * c + g + 1))
                        if c:
                            pe.wait_ge(vn_ok, t * 4 + (1 + g))
                        for h in range(GH * g, GH * g + GH):
                            m = pe.matmul(heads(4)[:, h, :], T[own, h, :], R[own, h, :],
                                          start=h % GH == 0, stop=True, skip_group_check=True)
                        m.then_inc(vn_mm, 1)
                    for g in range(HALVES):
                        pe.wait_ge(vn_ok, t * 4 + (2 * c + g + 1))
                        for h in range(GH * g, GH * g + GH):
                            m = pe.matmul(heads(6)[:, h, :], TAILK[own, h, :], VN[own, h, :],
                                          start=h % GH == 0, stop=True, skip_group_check=True)
                        m.then_inc(su_mm, 1)
                        for h in range(GH * g, GH * g + GH):
                            m = pe.matmul(heads(2)[other, h, :], INT[own, h, p0:p0 + C], VN[own, h, :],
                                          start=False, stop=True, skip_group_check=True)
                        m.then_inc(o_mm, 1)
                block_f(B_DN + 3, t)
                pe.wait_ge(on_ok, t + 1)
                for h in range(NH):
                    m = pe.transpose(heads(2)[:, h, :], O[:, h, :], const["ident"])
                m.then_inc(on_mm, 1)
                pe.wait_ge(yd_ok, t * 2 + 2)
                pe.wait_ge(s_upd, t * 4 + 4)

            block_f(B_KV)
            block_f(B_KV + 1)

            def attend(n, c, s, before):
                pe.wait_ge(qs_ok, n + 1)
                pe.wait_ge(kvs_ok, n + 1)
                if before:
                    pe.wait_ge(ya_ok, n)
                for e in range(2):
                    for r in range(4):
                        m = pe.matmul(ps[:, 2 + e, 128 * r:128 * r + 128],
                                      qs[c][64 * e:64 * e + 64, 2 * r:2 * r + 2, :].rearrange("p a b -> p (a b)"),
                                      kvs[c][64 * e:64 * e + 64, r // 2, :], start=r == 0, stop=True,
                                      skip_group_check=True)
                m.then_inc(sc_mm, 1)
                pe.transpose(ps[:, 7, 0:128], kvs[c][:, 2, :], const["ident"]).then_inc(vw_mm, 1)
                block_f(B_GATE + 2 * c, s)
                block_f(B_GATE + 2 * c + 1, s)
                pe.wait_ge(pn_ok, n + 1)
                for a in range(8):
                    m = pe.transpose(heads(4)[:, a, :], PR[:, a, :], const["ident"])
                m.then_inc(pt_mm, 1)
                pe.wait_ge(vw_ok, n + 1)
                pe.wait_ge(pt_ok, n + 1)
                for e in range(2):
                    for j in range(2):
                        m = pe.matmul(ps[64 * e:64 * e + 64, 6, 256 * j:256 * j + 256], vt2[c][:, 64 * j:64 * j + 64],
                                      PT[:, 4 * e + 2 * j:4 * e + 2 * j + 2, :], start=j == 0, stop=True,
                                      skip_group_check=True)
                m.then_inc(pv_mm, 1)

            attend(0, 0, 0, False)
            attend(1, 1, 0, True)
            with pe.Fori(1, S // P) as s:
                for c in range(2):
                    attend(s * 2 + c, c, s, True)

            for b0, tiles in ((B_BRA, 8), (B_BRD, 16)):
                for k in range(N_BR):
                    block_f(b0 + k, 0, tiles if k == 0 else None)
            pe.wait_ge(blk_read, B_OUT)
            for k in range(N_OUT):
                pe.wait_ge(a_ok, 24 + k + 1)
                block_t(B_OUT + k, 0, k, k == 0, k == N_OUT - 1)
            pe.wait_ge(x1_ok, TT)
            transposes_in(TT)
            block_f(B_UP, 0, 32)
            for k in range(1, WS):
                block_f(B_UP + k)
            with pe.Fori(0, N_UP // WS - 1) as i:
                for k in range(WS):
                    block_f(B_UP + WS + k, i)
            pe.wait_ge(blk_read, B_DOWN - N_OUT)

            def down(i, first=False, last=False):
                for k in range(WS):
                    pe.wait_ge(a_ok, i * WS + (40 + k + 1))
                    block_t(B_DOWN + k, i, k, first and k == 0, last and k == WS - 1)

            down(0, first=True)
            with pe.Fori(1, N_DOWN // WS - 1) as i:
                down(i)
            down(N_DOWN // WS - 1, last=True)

        @block.scalar
        def _(act):
            def hi(b, i=0):
                act.wait_ge(raw_in[b % RS], i * (16 * WS // RS) + 16 * (b // RS + 1))
                if b >= WS:
                    act.wait_ge(blk_mm, i * WS + (b - WS + 1))
                act.activation(w_hi[:, b % WS, :], raw[:, b % RS, :], ACT.Copy).then_inc(w_hi_ok, 1)

            def row_scales(done):
                act.wait_ge(ss_ok, done + TT)
                act.activation(rstd, ss, ACT.Ln, bias=eps_c, scale=1.0 / D).then_inc(ln_ok, 1)
                act.wait_ge(ln_ok, done // TT + 1)
                act.activation(rstd, rstd, ACT.Exp, scale=-0.5).then_inc(rstd_ok, 1)

            def norm_hi(done, row):
                for k in range(KT):
                    act.activation(act_hi[:, k, :], ps[:, k, :], ACT.Identity,
                                   scale=par[:, row + k:row + k + 1]).then_inc(a_hi_ok, 1)

            act.preload_act_table_set("natural_log_exp_and_others")
            act.wait_ge(eps_ok, 1)
            for t in range(TT):
                act.wait_ge(x_in, 16 * TT)
                act.activation(flat(O_JUNK0 + D * t, D), xn[:, t, :], ACT.Square, accum_out=ss[:, t:t + 1]).then_inc(ss_ok, 1)
            row_scales(0)
            for b in range(WS):
                hi(b)
            act.wait_ge(wb_in, 16)
            act.activation(wb_hi[:, :], wbeta, ACT.Copy).then_inc(wb_hi_ok, 1)
            act.wait_ge(xt_mm, 1)
            act.wait_ge(par_ok, 1)
            norm_hi(0, PR_MIX)
            act.wait_ge(sm, 3)
            act.activation(tmp[1], tmp[1], ACT.Exp).then_inc(sm_act, 1)
            act.activation(beta3, bd_cols[:, :, 0:NH], ACT.Exp, scale=-1.0).then_inc(sm_act, 1)
            act.wait_ge(small_in, 4 * 16)
            act.activation(alog, alog, ACT.Exp).then_inc(sm_act, 1)
            act.wait_ge(sm_act, 1)
            act.activation(tmp[1], tmp[1], ACT.Ln, bias=1.0).then_inc(sm_act, 1)
            with act.Fori(0, N_CONV // WS) as i:
                for k in range(WS):
                    act.wait_ge(blk_read, i * WS + (k + 1))
                    apart(act)
                    q = qkv[:, bass.ds(i * WS + k, 1), :]
                    act.activation(q, q, ACT.Silu).then_inc(conv_ok, 1)
                    hi(WS + k, i)
            act.preload_act_table_set("natural_log_exp_and_others")
            act.wait_ge(gc_mm, 1)
            act.activation(tail, ps[:, 4, 0:32], ACT.Exp).then_inc(gc_ok, 1)
            act.wait_ge(conv_ok, N_CONV)

            def filler(t, k):
                act.wait_ge(blk_mm, t * WS + (B_DN + k + 1))
                apart(act)
                act.activation(qkv[:, 4 * k:4 * k + 4, bass.ds(t * 128, 128)],
                               ps[:, k % 2, :].rearrange("p (a n) -> p a n", a=4), ACT.Copy).then_inc(blk_read, 1)
                hi(B_DN + WS + k, t)

            with act.Fori(0, TT) as t:
                now = bass.ds(t * 128, 128)
                for n in range(2):
                    act.activation((X, T)[n], qkv[:, 8 - 8 * n:16 - 8 * n, now], ACT.Square).then_inc(sq_ok, 1)
                for n in range(2):
                    act.wait_ge(ss_mm, t * 2 + (n + 1))
                    act.activation((X, T)[n], heads(2 + 2 * n), ACT.Ln, bias=eps_c).then_inc(lns_ok, 1)
                act.wait_ge(arg_ok, t + 1)
                act.activation(EG, heads(6), ACT.Exp).then_inc(eg_ok, 1)
                for n in range(2):
                    act.wait_ge(lns_ok, t * 2 + (n + 1))
                    act.activation((X, T)[n], (X, T)[n], ACT.Exp, scale=-0.5,
                                   bias=(zero_c, lnq_c)[n]).then_inc(rn_ok, 1)
                act.activation(VS, qkv[:, 16:24, now], ACT.Copy).then_inc(vs_ok, 1)
                for n in range(2):
                    act.wait_ge(darg_ok, t * 2 + (n + 1))
                    act.activation((L, INT)[n], (L, INT)[n], ACT.Exp).then_inc(dexp_ok, 1)
                act.wait_ge(kq_ok, t * 2 + 2)
                filler(t, 0)
                filler(t, 1)
                act.wait_ge(vt_mm, t + 1)
                act.activation(VTOK, heads(2), ACT.Copy).then_inc(vtok_ok, 1)
                act.wait_ge(lt_mm, t + 1)
                act.activation(LT, heads(6), ACT.Copy).then_inc(lt_ok, 1)
                filler(t, 2)
                for c in range(2):
                    other = slice(C - C * c, 2 * C - C * c)
                    own = slice(C * c, C * c + C)
                    for g in range(HALVES):
                        hs = slice(GH * g, GH * g + GH)
                        act.wait_ge(vn_mm, t * 4 + (2 * c + g + 1))
                        act.activation(VN[own, hs, :], heads(4)[own, hs, :], ACT.Copy).then_inc(vn_ok, 1)
                    for g in range(HALVES):
                        hs = slice(GH * g, GH * g + GH)
                        act.wait_ge(o_mm, t * 4 + (2 * c + g + 1))
                        act.activation(O[other, hs, :], heads(2)[other, hs, :], ACT.Copy).then_inc(o_ok, 1)
                act.wait_ge(oss_ok, t + 1)
                act.activation(ors, oss, ACT.Ln, scale=1.0 / 128, bias=eps_c).then_inc(oln_ok, 1)
                act.wait_ge(oln_ok, t + 1)
                act.activation(ors, ors, ACT.Exp, scale=-0.5).then_inc(ors_ok, 1)
                filler(t, 3)
                act.wait_ge(on_mm, t + 1)
                apart(act)
                for c in range(2):
                    act.activation(yd[:, :, bass.ds(t * 128 + C * c, C)], heads(2)[:, :, C - C * c:2 * C - C * c],
                                   ACT.Identity, scale=dnw).then_inc(yd_ok, 1)

            act.wait_ge(kv_pad, 1)
            act.wait_ge(blk_mm, B_KV + 1)
            for j in range(2):
                for e in range(2):
                    act.activation(kvt[64 * e:64 * e + 64, j, C:], ps[64 * j:64 * j + 64, 0, :],
                                   ACT.Copy).then_inc(kv_ok, 1)
            act.wait_ge(kv_ok, 4)
            act.activation(kvt[0:1, 0, 0:1], kvt[0:1, 0, 0:1], ACT.Copy).then_inc(blk_read, 1)
            hi(B_KV + WS)
            act.wait_ge(blk_mm, B_KV + 2)
            act.activation(kvt[:, 2, C:], ps[:, 1, :], ACT.Copy).then_inc(blk_read, 1)
            hi(B_KV + WS + 1)
            act.wait_ge(yd_ok, 2 * TT)
            for j in range(2):
                act.activation(qkv[:, 4 * j:4 * j + 4, :], qkv[:, 4 * j:4 * j + 4, :], ACT.Silu).then_inc(dz_ok, 1)
            act.preload_act_table_set("exp_and_others")
            act.wait_ge(blk_read, B_KV + 2)

            queries = arena[:, QKV:QKV + 24 * S].rearrange("p (b s t u q) -> p b s t u q", b=6, s=4, t=4, u=2)

            def attend(n, c, s):
                act.activation(qs[c].rearrange("p (t j) q -> p j t q", j=2),
                               queries[:, 2:4, bass.ds(s, 1), :, c, :].rearrange("p b s t q -> p b (s t) q"),
                               ACT.Copy).then_inc(qs_ok, 1)
                act.activation(kvs[c], kvt[:, :, bass.ds(n * C, 128)], ACT.Copy).then_inc(kvs_ok, 1)
                act.wait_ge(vw_mm, n + 1)
                act.activation(vt2[c], ps[:, 7, 0:128], ACT.Copy).then_inc(vw_ok, 1)
                act.wait_ge(pe_ok, n + 1)
                act.activation(PR, PR, ACT.Exp).then_inc(exp_ok, 1)
                act.wait_ge(esd_ok, n + 1)
                act.activation(es, es, ACT.Exp).then_inc(es_ok, 1)
                hi(B_GATE + WS + 2 * c, s)
                hi(B_GATE + WS + 2 * c + 1, s)
                act.wait_ge(pv_mm, n + 1)
                apart(act)
                act.activation(yatt[:, :, bass.ds(n * C, C)], ps[:, 6, :].rearrange("p (h q) -> p h q", h=KT),
                               ACT.Copy).then_inc(ya_ok, 1)

            with act.Fori(0, S // P) as s:
                for c in range(2):
                    attend(s * 2 + c, c, s)

            act.wait_ge(ya_ok, S // C)
            act.wait_ge(blk_mm, B_BRA)
            for k in range(KT):
                act.activation(act_hi[:, k, :], yatt[:, k, :], ACT.Copy).then_inc(a_hi_ok, 1)
            act.wait_ge(blk_read, B_BRA)
            act.activation(gates[:, 0:8, :], gates[:, 0:8, :], ACT.Sigmoid).then_inc(sig_ok, 1)
            hi(B_BRA + WS)
            act.activation(gates[:, 8:16, :], gates[:, 8:16, :], ACT.Sigmoid).then_inc(sig_ok, 1)
            for k in range(1, N_BR):
                hi(B_BRA + WS + k)
            act.wait_ge(ydz_ok, 4)
            act.wait_ge(blk_mm, B_BRD)
            for k in range(KT):
                act.activation(act_hi[:, k, :], yd[:, k, :], ACT.Copy).then_inc(a_hi_ok, 1)
            for k in range(N_BR):
                hi(B_BRD + WS + k)
            act.wait_ge(blk_mm, B_OUT)
            for k in range(KT):
                act.wait_ge(mg_ok, k + 1)
                act.activation(act_hi[:, k, :], gates[:, k, :], ACT.Copy).then_inc(a_hi_ok, 1)
            for k in range(N_OUT):
                hi(B_OUT + WS + k)
            act.preload_act_table_set("natural_log_exp_and_others")
            for t in range(TT):
                act.wait_ge(x1_ok, t + 1)
                act.activation(flat(O_JUNK1 + D * t, D), x1[:, t, :], ACT.Square, accum_out=ss[:, t:t + 1]).then_inc(ss_ok, 1)
            row_scales(TT)
            act.wait_ge(xt_mm, 2)
            norm_hi(TT, PR_MLP)
            with act.Fori(0, N_UP // WS) as i:
                for k in range(WS):
                    act.wait_ge(blk_mm, i * WS + (B_UP + k + 1))
                    apart(act)
                    act.activation(a_t[:, bass.ds(i * WS + k, 1), :].rearrange("p a n -> p (a n)"), ps[:, k % 2, :],
                                   ACT.Relu).then_inc(relu_ok, 1)
                    hi(B_UP + WS + k, i)

            def squares_hi(k, i=0):
                act.wait_ge(blk_read, i * WS + (B_UP - N_OUT + k + 1))
                act.wait_ge(blk_mm, i * WS + (B_DOWN + k - WS + 1) if k >= WS else B_DOWN)
                apart(act)
                act.activation(act_hi[:, k % WS, :], a_t[:, bass.ds(i * WS + k, 1), :].rearrange("p a n -> p (a n)"),
                               ACT.Copy).then_inc(a_hi_ok, 1)

            for k in range(WS):
                squares_hi(k)
            with act.Fori(0, N_DOWN // WS - 1) as i:
                for k in range(WS):
                    hi(B_DOWN + WS + k, i)
                    squares_hi(WS + k, i)
            for t in range(TT):
                act.wait_ge(y_add, t + 1)
                act.activation(flat(O_JUNK1 + D * t, D), x1[:, t, :], ACT.Square, accum_out=ss[:, t:t + 1]).then_inc(ss_ok, 1)
            row_scales(2 * TT)

        @block.vector
        def _(dve):
            def norm_lo(done, row):
                for k in range(KT):
                    dve.wait_ge(a_hi_ok, done + k + 1)
                    dve.scalar_tensor_tensor(out=act_lo[:, k, :], in0=ps[:, k, :], scalar=par[:, row + k:row + k + 1],
                                             in1=act_hi[:, k, :].bitcast(F32), op0=ALU.mult,
                                             op1=ALU.subtract).then_inc(a_ok, 1)

            def split_lo(done, src):
                for k in range(KT):
                    dve.wait_ge(a_hi_ok, done + k + 1)
                    dve.tensor_tensor(act_lo[:, k, :], src[:, k, :], act_hi[:, k, :].bitcast(F32),
                                      ALU.subtract).then_inc(a_ok, 1)

            dve.memset(eps_c, EPS)
            dve.memset(zero_c, 0.0)
            dve.memset(lnq_c, LN_Q_SCALE).then_inc(eps_ok, 1)
            dve.wait_ge(par_mm, 1)
            dve.tensor_copy(par, ps[:, 0, 0:128]).then_inc(par_ok, 1)
            dve.wait_ge(rstd_ok, 1)
            for t in range(TT):
                dve.tensor_scalar(xn[:, t, :], xn[:, t, :], rstd[:, t:t + 1], None, ALU.mult).then_inc(xn_ok, 1)
            dve.wait_ge(wb_hi_ok, 1)
            dve.tensor_tensor(wb_lo[:, :], wbeta, wb_hi[:, :].bitcast(F32), ALU.subtract).then_inc(wb_ok, 1)
            dve.wait_ge(par_ok, 1)
            norm_lo(0, PR_MIX)
            dve.wait_ge(bd_mm, 1)
            dve.tensor_copy(bd_rows, ps[0:2 * NH, 2, :]).then_inc(bd_ok, 1)
            dve.wait_ge(bdt_mm, 1)
            dve.wait_ge(small_in, 4 * 16)
            y3, z3 = (a.rearrange("p (t h) -> p t h", h=NH) for a in tmp)

            def rows(a):
                return a.unsqueeze(1).to_broadcast([P, TT, NH])

            dve.tensor_tensor(y3, bd_cols[:, :, NH:2 * NH], rows(dtb), ALU.add).then_inc(sm, 1)
            dve.wait_ge(sm, 1)
            dve.tensor_scalar(tmp[1], tmp[0], -1.0, None, ALU.mult).then_inc(sm, 1)
            dve.wait_ge(sm, 2)
            dve.tensor_tensor(tmp[1], tmp[0], tmp[1], ALU.min).then_inc(sm, 1)
            dve.wait_ge(sm_act, 4)
            dve.wait_ge(sm, 3)
            dve.scalar_tensor_tensor(out=tmp[0], in0=tmp[0], scalar=0.0, in1=tmp[1], op0=ALU.max,
                                     op1=ALU.add).then_inc(sm, 1)
            dve.tensor_scalar(beta, beta, 1.0, None, ALU.add).then_inc(sm, 1)
            dve.wait_ge(sm, 5)
            dve.scalar_tensor_tensor(out=dec3, in0=y3, scalar=-1.0, in1=rows(alog), op0=ALU.mult,
                                     op1=ALU.mult).then_inc(g_ok, 1)
            dve.reciprocal(beta, beta).then_inc(sm, 1)
            for hl in range(2):
                rs = slice(64 * hl, 64 * hl + 64)
                dve.tensor_copy(sinks[rs, :].rearrange("p (e r) -> p e r", e=2),
                                sinks_all[rs, :].rearrange("p (r l e) -> p l e r", l=2, e=2)[:, hl]).then_inc(sink_ok, 1)
            with dve.Fori(0, N_CONV // WS) as i:
                for k in range(WS):
                    dve.wait_ge(blk_mm, i * WS + (k + 1))
                    q = qkv[:, bass.ds(i * WS + k, 1), :].rearrange("p a n -> p (a n)")
                    z = ps[:, k % 2, :]
                    taps = [par[:, bass.ds(i * WS + (PR_CONV + 24 * j + k), 1)] for j in range(4)]
                    dve.tensor_scalar(q, z, taps[3], None, ALU.mult).then_inc(conv_tap, 1)
                    for j in (2, 1, 0):
                        d = 3 - j
                        dve.wait_ge(conv_tap, i * (3 * WS) + (3 * k + d))
                        m = dve.scalar_tensor_tensor(out=q[:, d:S], in0=z[:, 0:S - d], scalar=taps[j],
                                                     in1=q[:, d:S], op0=ALU.mult, op1=ALU.add)
                        m.then_inc(conv_tap if j else blk_read, 1)
            dve.memset(arena[:, O_S:O_S + 1024], 0.0).then_inc(s0_ok, 1)
            dve.wait_ge(gc_mm, 1)
            dve.tensor_copy(gcol, ps[:, 3, 0:32]).then_inc(gc_ok, 1)
            dve.wait_ge(sm, 6)
            dve.wait_ge(gc_ok, 2)

            with dve.Fori(0, TT) as t:
                now = bass.ds(t * 128, 128)

                def token_col(a3):
                    return col(a3[:, bass.ds(t, 1), :].rearrange("p a h -> p (a h)"))

                dve.tensor_copy(g_now, dec3[:, bass.ds(t, 1), :].rearrange("p a h -> p (a h)")).then_inc(g_now_ok, 1)
                dve.wait_ge(grow_mm, t + 1)
                dve.tensor_tensor(INT, heads(6), token_col(gcol3), ALU.subtract).then_inc(arg_ok, 1)
                dve.wait_ge(arg_ok, t + 1)
                dve.tensor_tensor(L, mat("mask_l"), INT, ALU.subtract).then_inc(darg_ok, 1)
                dve.tensor_tensor(INT, mat("mask_t"), INT, ALU.add).then_inc(darg_ok, 1)
                dve.wait_ge(eg_ok, t + 1)
                dve.tensor_copy(gl3, EG[:, :, C - 1:2 * C:C]).then_inc(gl_ok, 1)
                for n in range(2):
                    dve.wait_ge(rn_ok, t * 2 + (n + 1))
                    dve.tensor_tensor(KQ[:, :, n, :], qkv[:, 8 - 8 * n:16 - 8 * n, now], (X, T)[n],
                                      ALU.mult).then_inc(kq_ok, 1)
                grams = ps[:, 2:6, :].rearrange("p b (h s n) -> p (b h) s n", h=2, s=2)
                dve.wait_ge(gram_mm, t + 1)
                dve.wait_ge(dexp_ok, t * 2 + 1)
                dve.tensor_tensor(L, grams[:, :, 0, :], L, ALU.mult).then_inc(l_raw, 1)
                dve.wait_ge(dexp_ok, t * 2 + 2)
                dve.tensor_tensor(INT, grams[:, :, 1, :], INT, ALU.mult).then_inc(int_ok, 1)
                dve.wait_ge(l_raw, t + 1)
                dve.tensor_tensor(L, L, token_col(beta3), ALU.mult).then_inc(l_ok, 1)
                dve.wait_ge(l_ok, t + 1)
                dve.tensor_tensor(Y, L, mat("m1"), ALU.mult).then_inc(y1_ok, 1)
                dve.wait_ge(y1_ok, t + 1)
                dve.tensor_tensor(X, mat("ident"), Y, ALU.subtract).then_inc(x0_ok, 1)
                dve.wait_ge(kt_mm, t + 1)
                dve.wait_ge(lt_mm, t + 1)
                dve.tensor_tensor(TAILK, heads(4), token_col(tail3), ALU.mult).then_inc(kdec_ok, 1)
                dve.wait_ge(lt_ok, t + 1)
                dve.wait_ge(x0_ok, t + 1)
                dve.tensor_tensor(Y, LT, mat("m1t"), ALU.mult).then_inc(y2_ok, 1)
                dve.wait_ge(y2_ok, t + 1)
                dve.tensor_tensor(T, mat("ident"), Y, ALU.subtract).then_inc(t0_ok, 1)
                for lv, name in enumerate(LEVELS):
                    for g in range(HALVES):
                        hs = slice(GH * g, GH * g + GH)
                        dve.wait_ge(y_mm, t * 10 + (2 * lv + g + 1))
                        if lv == 0 and g == 0:
                            dve.wait_ge(t0_ok, t + 1)
                        dve.tensor_tensor(Y[:, hs, :], heads(2)[:, hs, :], mat(name, GH), ALU.mult).then_inc(y_ok, 1)
                    for g in range(HALVES):
                        hs = slice(GH * g, GH * g + GH)
                        dve.wait_ge(xt2_mm, t * 10 + (2 * lv + g + 1))
                        if lv < len(LEVELS) - 1:
                            dve.tensor_tensor(X[:, hs, :], X[:, hs, :], heads(4)[:, hs, :], ALU.subtract).then_inc(x_upd, 1)
                        dve.tensor_tensor(T[:, hs, :], T[:, hs, :], heads(6)[:, hs, :], ALU.subtract).then_inc(t_upd, 1)
                dve.wait_ge(t_upd, t * 10 + 10)
                dve.tensor_tensor(T, T, token_col(beta3), ALU.mult).then_inc(tb_ok, 1)
                for c in range(2):
                    own = slice(C * c, C * c + C)
                    for g in range(HALVES):
                        hs = slice(GH * g, GH * g + GH)
                        dve.wait_ge(kq_mm, t * 4 + (2 * c + g + 1))
                        dve.wait_ge(vtok_ok, t + 1)
                        dve.tensor_tensor(R[own, hs, :], VTOK[own, hs, :], heads(2)[own, hs, :],
                                          ALU.subtract).then_inc(r_ok, 1)
                    for g in range(HALVES):
                        dve.wait_ge(su_mm, t * 4 + (2 * c + g + 1))
                        dve.wait_ge(gl_ok, t + 1)
                        for h in range(GH * g, GH * g + GH):
                            m = dve.scalar_tensor_tensor(out=ST[:, h, :], in0=ST[:, h, :], scalar=gl3[:, h, c:c + 1],
                                                         in1=heads(6)[:, h, :], op0=ALU.mult, op1=ALU.add)
                        m.then_inc(s_upd, 1)
                dve.wait_ge(o_ok, t * 4 + 4)
                dve.tensor_tensor(Y, O, O, ALU.mult).then_inc(osq_ok, 1)
                dve.wait_ge(osq_ok, t + 1)
                dve.tensor_reduce(oss, Y, AX_X, ALU.add).then_inc(oss_ok, 1)
                dve.wait_ge(ors_ok, t + 1)
                dve.tensor_tensor(O, O, col(ors), ALU.mult).then_inc(on_ok, 1)

            dve.memset(kvt[:, :, 0:C], 0.0).then_inc(kv_pad, 1)
            for j in range(2):
                dve.wait_ge(dz_ok, j + 1)
                dve.wait_ge(yd_ok, 2 * TT)
                for half in range(2):
                    y = arena[:, YD:YD + NH * S].rearrange("p (t j s n) -> p t j s n", t=4, j=2, s=4)[:, :, j, 2 * half:2 * half + 2, :]
                    z = arena[:, QKV + 4 * j * S:QKV + 4 * (j + 1) * S].rearrange("p (s t n) -> p t s n", s=4, t=4)[:, :, 2 * half:2 * half + 2, :]
                    dve.tensor_tensor(y, y, z, ALU.mult).then_inc(ydz_ok, 1)

            def attend(n, c, s, first):
                k0 = C if first else 0
                sc = heads(2)[:, :, k0:]
                prk = PR[:, :, k0:]
                w = 128 - k0
                dve.wait_ge(sc_mm, n + 1)
                dve.tensor_reduce(mx, sc, AX_X, ALU.max).then_inc(mx_ok, 1)
                dve.wait_ge(mx_ok, n + 1)
                dve.scalar_tensor_tensor(out=mx, in0=mx, scalar=HD ** -0.5, in1=sinks, op0=ALU.mult,
                                         op1=ALU.max).then_inc(m_ok, 1)
                dve.wait_ge(m_ok, n + 1)
                dve.scalar_tensor_tensor(out=prk, in0=sc, scalar=HD ** -0.5,
                                         in1=mx.unsqueeze(2).to_broadcast([P, 8, w]), op0=ALU.mult,
                                         op1=ALU.subtract).then_inc(pe_ok, 1)
                dve.tensor_tensor(es, sinks, mx, ALU.subtract).then_inc(esd_ok, 1)
                dve.wait_ge(exp_ok, n + 1)
                if first:
                    dve.memset(PR[:, :, 0:C], 0.0)
                dve.tensor_reduce(den, prk, AX_X, ALU.add).then_inc(den_ok, 1)
                dve.wait_ge(es_ok, n + 1)
                dve.wait_ge(den_ok, n * 2 + 1)
                dve.tensor_tensor(den, den, es, ALU.add).then_inc(den_ok, 1)
                dve.wait_ge(den_ok, n * 2 + 2)
                dve.reciprocal(den, den).then_inc(rden_ok, 1)
                for k in range(2):
                    dve.wait_ge(blk_mm, s * WS + (B_GATE + 2 * c + k + 1))
                    dve.tensor_scalar(gates[:, bass.ds(s * WS + (2 * c + k), 1), :].rearrange("p a n -> p (a n)"),
                                      ps[:, k, :], par[:, bass.ds(s * WS + (PR_GATE + 2 * c + k), 1)], None,
                                      ALU.add).then_inc(blk_read, 1)
                dve.wait_ge(pt_mm, n + 1)
                dve.tensor_copy(PT, heads(4)).then_inc(pt_ok, 1)

            dve.wait_ge(sink_ok, 2)
            attend(0, 0, 0, True)
            attend(1, 1, 0, False)
            with dve.Fori(1, S // P) as s:
                for c in range(2):
                    attend(s * 2 + c, c, s, False)

            dve.wait_ge(ya_ok, S // C)
            split_lo(8, yatt)
            dve.wait_ge(sig_ok, 1)
            for k in range(N_BR):
                dve.wait_ge(blk_mm, B_BRA + k + 1)
                dve.tensor_tensor(gates[:, k, :], gates[:, k, :], ps[:, k % 2, :], ALU.mult).then_inc(blk_read, 1)
            dve.wait_ge(sig_ok, 2)
            split_lo(16, yd)
            for k in range(N_BR):
                dve.wait_ge(blk_mm, B_BRD + k + 1)
                dve.tensor_tensor(gates[:, 8 + k, :], gates[:, 8 + k, :], ps[:, k % 2, :], ALU.mult).then_inc(blk_read, 1)
                dve.wait_ge(blk_read, B_BRD + k + 1)
                dve.tensor_tensor(gates[:, k, :], gates[:, k, :], gates[:, 8 + k, :], ALU.add).then_inc(mg_ok, 1)
            split_lo(24, gates)
            dve.wait_ge(x_again, 16)
            dve.wait_ge(blk_mm, B_UP)
            for t in range(TT):
                dve.tensor_tensor(x1[:, t, :], x1[:, t, :], ps[:, 2 * t:2 * t + 2, :].rearrange("p b n -> p (b n)"),
                                  ALU.add).then_inc(x1_ok, 1)
            dve.wait_ge(rstd_ok, 2)
            for t in range(TT):
                dve.tensor_scalar(xn[:, t, :], x1[:, t, :], rstd[:, t:t + 1], None, ALU.mult).then_inc(xn_ok, 1)
            norm_lo(32, PR_MLP)
            with dve.Fori(0, N_UP // WS) as i:
                for k in range(WS):
                    dve.wait_ge(relu_ok, i * WS + (k + 1))
                    a = a_t[:, bass.ds(i * WS + k, 1), :].rearrange("p a n -> p (a n)")
                    dve.tensor_tensor(a, a, ps[:, k % 2, :], ALU.mult).then_inc(blk_read, 1)
            with dve.Fori(0, N_DOWN // WS) as i:
                for k in range(WS):
                    dve.wait_ge(a_hi_ok, i * WS + (40 + k + 1))
                    dve.tensor_tensor(act_lo[:, k, :], a_t[:, bass.ds(i * WS + k, 1), :].rearrange("p a n -> p (a n)"),
                                      act_hi[:, k, :].bitcast(F32), ALU.subtract).then_inc(a_ok, 1)
            dve.wait_ge(blk_mm, B_END)
            for t in range(TT):
                dve.tensor_tensor(x1[:, t, :], x1[:, t, :], ps[:, 2 * t:2 * t + 2, :].rearrange("p b n -> p (b n)"),
                                  ALU.add).then_inc(y_add, 1)
            dve.wait_ge(rstd_ok, 3)
            dve.wait_ge(fw_ok, 16)
            for t in range(TT):
                dve.scalar_tensor_tensor(out=x1[:, t, :], in0=x1[:, t, :], scalar=rstd[:, t:t + 1], in1=fw,
                                         op0=ALU.mult, op1=ALU.mult).then_inc(y_fin, 1)


INPUTS = ["x", "norm_mix_w", "w_in", "b_gate", "attn_sinks", "conv_w", "a_log", "dt_bias", "dn_norm_w",
          "w_branch_attn", "w_branch_delta", "w_out", "norm_mlp_w", "w_mlp_up", "w_mlp_down", "final_norm_w"]


def shape_constants(np):
    i, j = np.arange(P)[:, None], np.arange(P)[None, :]
    same = i // C == j // C
    level = {b: (i // (2 * b) == j // (2 * b)) & (i % (2 * b) >= b) & (j % (2 * b) < b) for b in (1, 2, 4, 8, 16, 32)}
    mats = {"ident": i == j, "ones": np.ones((P, P)), "tri": same & (i <= j), "later": same & (i > j),
            "mask_t": np.where(same & (j >= i), 0.0, NEG), "mask_l": np.where(same & (i > j), 0.0, NEG),
            "m1": level[1], "m1t": level[1].T, **{f"m{b}": level[b] for b in (2, 4, 8, 16, 32)}}
    return np.ascontiguousarray(np.stack([mats[n] for n in CONSTS], axis=1).astype(np.float32))


def kernel(**inputs):
    import numpy as np
    import concourse.bacc as bacc
    from concourse.bass_utils import run_bass_kernel_spmd

    nc = bacc.Bacc("TRN2", target_bir_lowering=False, num_devices=1)
    arrays = {f"in_{n}": np.ascontiguousarray(inputs[n]) for n in INPUTS}
    arrays["in_shape_consts"] = shape_constants(np)
    args = [nc.dram_tensor(n, a.shape, mybir.dt.from_np(a.dtype), kind="ExternalInput").ap() for n, a in arrays.items()]
    args.append(nc.dram_tensor("out_0", (1, S, D), F32, kind="ExternalOutput").ap())
    build(nc, *args)
    return run_bass_kernel_spmd(nc, [arrays], core_ids=[0]).results[0]["out_0"]
```

```python
import math
from contextlib import ExitStack

import concourse.bass as bass
from concourse import mybir
from concourse.alu_op_type import AluOpType as ALU

F32 = mybir.dt.float32
F32R = mybir.dt.float32r
ACT = mybir.ActivationFunctionType
AX_X = mybir.AxisListType.X

P = 128
D = 1024
S = 512
KT = D // P
TT = S // P
C = 64
HD = 64
NH = 8
FF = 4096
EPS = 1e-6
LN_Q_SCALE = -0.5 * math.log(128)
NEG = -1e30
HALVES = 2
GH = NH // HALVES

COL_Q, COL_K, COL_V, COL_CONV = 0, 1024, 1152, 1280
COL_BETA = COL_CONV + 3 * D
COL_DZ = COL_BETA + 2 * NH
COL_GATE = COL_DZ + D

N_CONV, N_DN, N_KV, N_GATE, N_BR, N_OUT, N_UP, N_DOWN = 24, 16, 2, 16, 8, 8, 32, 32
B_CONV = 0
B_DN = B_CONV + N_CONV
B_KV = B_DN + N_DN
B_GATE = B_KV + N_KV
B_BRD = B_GATE + N_GATE
B_BRA = B_BRD + N_BR
B_OUT = B_BRA + N_BR
B_UP = B_OUT + N_OUT
B_DOWN = B_UP + N_UP
B_END = B_DOWN + N_DOWN
WS = 4
RS = 2

PR_CONV, PR_MIX, PR_GATE, PR_MLP = 0, 96, 104, 120

CONSTS = ["ident", "ones", "tri", "later", "mask_t", "mask_l", "m1", "m2", "m4", "m8", "m16", "m32"]
LEVELS = ["m2", "m4", "m8", "m16", "m32"]

QKV = 0
YD = 24 * S
W0 = YD + 8 * S
(O_KQ, O_KD, O_X, O_T, O_Y, O_LT, O_INT, O_L, O_VTOK, O_R, O_VN, O_S, O_O, O_END) = (
    W0 + 1024 * k for k in (0, 2, 4, 5, 6, 7, 8, 9, 10, 11, 12, 13, 14, 15))
O_GATES = W0
O_P, O_PT, O_QS = W0 + 8192, W0 + 9216, W0 + 10240
O_KVS, O_KVT, O_VT2 = W0 + 11264, W0 + 12032, W0 + 13760
O_YATT = QKV + 16 * S
O_XN, O_PROW, O_JUNK0 = W0, W0 + 5120, W0 + 6144
O_X1, O_FW, O_JUNK1 = W0 + 8192, W0 + 12288, W0 + 4096
O_CONST = O_END
O_PT_PAR = O_CONST + 128 * len(CONSTS)
O_SMALL = O_PT_PAR + 128
ARENA = O_SMALL + 512


def build(nc, x, norm_mix_w, w_in, b_gate, attn_sinks, conv_w, a_log, dt_bias, dn_norm_w,
          w_branch_attn, w_branch_delta, w_out, norm_mlp_w, w_mlp_up, w_mlp_down, final_norm_w,
          shape_consts, out):
    w_in_v = w_in[0].rearrange("(k p) n -> p k n", p=P)
    bra_v = w_branch_attn[0].rearrange("(k p) n -> p k n", p=P)
    brd_v = w_branch_delta[0].rearrange("(k p) n -> p k n", p=P)
    up_v = w_mlp_up[0].rearrange("(k p) n -> p k n", p=P)
    x_v = x[0].rearrange("(t p) n -> p t n", p=P)
    out_v = out[0].rearrange("(t p) n -> p t n", p=P)

    with ExitStack() as ctx:
        def sem(name):
            return ctx.enter_context(nc.semaphore(name))

        arena = ctx.enter_context(nc.sbuf_tensor("arena", [P, ARENA], F32))
        raw = ctx.enter_context(nc.sbuf_tensor("raw", [P, RS, D], F32))
        w_hi = ctx.enter_context(nc.sbuf_tensor("w_hi", [P, WS, D], F32R))
        w_lo = ctx.enter_context(nc.sbuf_tensor("w_lo", [P, WS, D], F32R))
        act_hi = ctx.enter_context(nc.sbuf_tensor("act_hi", [P, KT, S], F32R))
        act_lo = ctx.enter_context(nc.sbuf_tensor("act_lo", [P, KT, S], F32R))
        wb_hi = ctx.enter_context(nc.sbuf_tensor("wb_hi", [P, KT * 2 * NH], F32R))
        wb_lo = ctx.enter_context(nc.sbuf_tensor("wb_lo", [P, KT * 2 * NH], F32R))
        ps = ctx.enter_context(nc.psum_tensor("ps", [P, 8, 512], F32))

        def flat(off, n, p0=0, p1=P):
            return arena[p0:p1, off:off + n]

        def grid(off, a, b):
            return arena[:, off:off + a * b].rearrange("p (a b) -> p a b", a=a)

        def heads(bank):
            return ps[:, bank:bank + 2, :].rearrange("p b (h n) -> p (b h) n", n=128)

        qkv = grid(QKV, 24, S)
        yd = grid(YD, NH, S)
        KQ = arena[:, O_KQ:O_KQ + 2048].rearrange("p (h s n) -> p h s n", h=NH, s=2)
        KD = arena[:, O_KD:O_KD + 2048].rearrange("p (h c s n) -> p h c s n", h=NH, c=2, s=2)
        X, T, Y, LT, INT, L, VTOK, R, VN, ST, O = (
            grid(o, NH, 128) for o in (O_X, O_T, O_Y, O_LT, O_INT, O_L, O_VTOK, O_R, O_VN, O_S, O_O))
        EG, VS, TAILK = R, VN, L
        gates = grid(O_GATES, 16, S)
        PR, PT = grid(O_P, 8, 128), grid(O_PT, 8, 128)
        qs = [grid(O_QS + 512 * c, 8, C) for c in range(2)]
        kvs = [grid(O_KVS + 384 * c, 3, 128) for c in range(2)]
        kvt = grid(O_KVT, 3, S + C)
        vt2 = [flat(O_VT2 + 128 * c, 128) for c in range(2)]
        yatt = grid(O_YATT, KT, S)
        xn = grid(O_XN, TT, D)
        x1 = grid(O_X1, TT, D)
        fw = flat(O_FW, D)
        a_t = grid(0, N_UP, S)
        const = {n: flat(O_CONST + 128 * i, 128) for i, n in enumerate(CONSTS)}
        par = flat(O_PT_PAR, 128)

        at = [O_SMALL]

        def small(n):
            at[0] += n
            assert at[0] <= ARENA
            return flat(at[0] - n, n)

        ss, rstd = small(4), small(4)
        beta, dec, gcol, tail = small(32), small(32), small(32), small(32)
        alog, dtb = small(8), small(8)
        sinks, sinks_all = small(8), small(16)
        dnw = small(1)
        wbeta = small(KT * 2 * NH)
        g_now = small(8)
        gl = small(16)
        oss, ors = small(8), small(8)
        mx, es, den = small(8), small(8), small(8)
        tmp = [small(32), small(32)]
        eps_c, lnq_c, zero_c = small(1), small(1), small(1)
        beta3, dec3, gcol3, tail3 = (a.rearrange("p (t h) -> p t h", h=NH) for a in (beta, dec, gcol, tail))
        gl3 = gl.rearrange("p (h c) -> p h c", c=2)
        bd_cols = ps[:, 3, 0:TT * 2 * NH].rearrange("p (t n) -> p t n", t=TT)
        prow = flat(O_PROW, 128)
        bd_rows = arena[0:2 * NH, YD:YD + S]

        def mat(name, n=NH):
            return const[name].unsqueeze(1).to_broadcast([P, n, 128])

        def col(a, n=NH):
            return a.unsqueeze(2).to_broadcast([a.shape[0], n, 128])

        x_in = [sem(f"x_in{t}") for t in range(TT)]
        consts_in, params_in, small_in, wb_in, x_again, out_sent = map(
            sem, ["consts_in", "params_in", "small_in", "wb_in", "x_again", "out_sent"])
        raw_in = [sem(f"raw_in{i}") for i in range(RS)]
        w_hi_ok, w_ok, blk_mm, blk_read = map(sem, ["w_hi_ok", "w_ok", "blk_mm", "blk_read"])
        a_hi_ok, a_ok, a_free = sem("a_hi_ok"), sem("a_ok"), sem("a_free")
        par_mm, par_ok, ss_ok, ln_ok, rstd_ok, xn_ok, xt_mm = map(
            sem, ["par_mm", "par_ok", "ss_ok", "ln_ok", "rstd_ok", "xn_ok", "xt_mm"])
        wb_hi_ok, wb_ok, bd_mm, bd_ok, bdt_mm, sm, sm_act, g_ok, gc_mm, gc_ok, gt_ok = map(
            sem, ["wb_hi_ok", "wb_ok", "bd_mm", "bd_ok", "bdt_mm", "sm", "sm_act", "g_ok", "gc_mm", "gc_ok", "gt_ok"])
        conv_tap, conv_ok, eps_ok, sink_ok = sem("conv_tap"), sem("conv_ok"), sem("eps_ok"), sem("sink_ok")
        (sq_ok, ss_mm, lns_ok, rn_ok, g_now_ok, grow_mm, eg_ok, gl_ok, kq_ok, arg_ok, darg_ok, dexp_ok, gram_mm,
         l_raw, l_ok, int_ok, vs_ok, lt_mm, vt_mm, kt_mm, lt_ok, vtok_ok, y1_ok, x0_ok, t0_ok, kdec_ok,
         y_mm, y_ok, xt2_mm, x_upd, t_upd, tb_ok, kdq_ok, kq_mm, r_ok, vn_mm, vn_ok, o_mm, su_mm, s_upd, o_ok,
         osq_ok, oss_ok, oln_ok, ors_ok, on_ok, on_mm, yd_ok, s0_ok) = map(sem, [
            "sq_ok", "ss_mm", "lns_ok", "rn_ok", "g_now_ok", "grow_mm", "eg_ok", "gl_ok", "kq_ok", "arg_ok",
            "darg_ok", "dexp_ok", "gram_mm", "l_raw", "l_ok", "int_ok", "vs_ok", "lt_mm", "vt_mm", "kt_mm",
            "lt_ok", "vtok_ok", "y1_ok", "x0_ok", "t0_ok", "kdec_ok", "y_mm", "y_ok", "xt2_mm",
            "x_upd", "t_upd", "tb_ok", "kdq_ok", "kq_mm", "r_ok", "vn_mm", "vn_ok", "o_mm", "su_mm", "s_upd",
            "o_ok", "osq_ok", "oss_ok", "oln_ok", "ors_ok", "on_ok", "on_mm", "yd_ok", "s0_ok"])
        (dz_ok, ydz_ok, kv_pad, kv_ok, qs_ok, kvs_ok, sc_mm, vw_mm, vw_ok, mx_ok, m_ok, pe_ok, esd_ok, exp_ok,
         es_ok, den_ok, rden_ok, pn_ok, pt_mm, pt_ok, pv_mm, ya_ok) = map(sem, [
            "dz_ok", "ydz_ok", "kv_pad", "kv_ok", "qs_ok", "kvs_ok", "sc_mm", "vw_mm", "vw_ok", "mx_ok", "m_ok",
            "pe_ok", "esd_ok", "exp_ok", "es_ok", "den_ok", "rden_ok", "pn_ok", "pt_mm", "pt_ok", "pv_mm", "ya_ok"])
        sig_ok, relu_ok, mg_ok, rows_mm, x1_ok, y_add, y_fin, fw_ok = map(
            sem, ["sig_ok", "relu_ok", "mg_ok", "rows_mm", "x1_ok", "y_add", "y_fin", "fw_ok"])

        apart_sem = sem("apart")

        def apart(engine):
            engine.sem_inc(apart_sem, 1)

        block = ctx.enter_context(nc.Block())

        @block.sync
        def _(sp):
            def load(b, i, src):
                if b >= RS:
                    sp.wait_ge(w_ok, b + WS * i - RS + 1)
                    if not isinstance(i, int):
                        apart(sp)
                dst = raw[:, b % RS, :]
                if len(src.shape) == 3:
                    dst = dst.rearrange("p (k n) -> p k n", k=KT)
                sp.dma_start(dst, src).then_inc(raw_in[b % RS], 16)

            def cols(view, c):
                return view[:, :, bass.ds(c, 128)]

            cflat = arena[:, O_CONST:O_CONST + 128 * len(CONSTS)]
            for t in range(TT):
                sp.dma_start(xn[:, t, :], x_v[:, t, :]).then_inc(x_in[t], 16)
                if t == 1:
                    sp.dma_start(cflat, shape_consts.rearrange("p a b -> p (a b)")).then_inc(consts_in, 16)
            sp.dma_start(prow[PR_CONV:PR_MIX, :], conv_w[0].rearrange("t (b p) -> (t b) p", p=P)).then_inc(params_in, 16)
            sp.dma_start(prow[PR_MIX:PR_GATE, :], norm_mix_w[0].rearrange("(b p) -> b p", p=P)).then_inc(params_in, 16)
            sp.dma_start(prow[PR_GATE:PR_MLP, :], b_gate[0].rearrange("(b p) -> b p", p=P)).then_inc(params_in, 16)
            sp.dma_start(prow[PR_MLP:P, :], norm_mlp_w[0].rearrange("(b p) -> b p", p=P)).then_inc(params_in, 16)
            sp.dma_start(wbeta.rearrange("p (k n) -> p k n", k=KT),
                         w_in_v[:, :, COL_BETA:COL_BETA + 2 * NH]).then_inc(wb_in, 16)
            load(0, 0, cols(w_in_v, COL_CONV))
            load(1, 0, cols(w_in_v, COL_CONV + 128))
            sp.dma_start(alog, a_log[0:1, :].to_broadcast([P, NH])).then_inc(small_in, 16)
            sp.dma_start(dtb, dt_bias[0:1, :].to_broadcast([P, NH])).then_inc(small_in, 16)
            sp.dma_start(dnw, dn_norm_w.rearrange("a p -> p a")).then_inc(small_in, 16)
            sp.dma_start(sinks_all, attn_sinks[0:1, :].to_broadcast([P, 16])).then_inc(small_in, 16)
            for b in range(2, WS):
                load(b, 0, cols(w_in_v, COL_CONV + 128 * b))
            with sp.Fori(0, N_CONV // WS - 1) as i:
                for k in range(WS):
                    load(WS + k, i, cols(w_in_v, i * 512 + (COL_CONV + 512 + 128 * k)))
            with sp.Fori(0, TT) as t:
                for k, c in enumerate((COL_DZ, COL_DZ + 128, COL_Q, COL_Q + 128)):
                    load(B_DN + k, t, cols(w_in_v, t * 256 + c))
            load(B_KV, 0, cols(w_in_v, COL_K))
            load(B_KV + 1, 0, cols(w_in_v, COL_V))
            with sp.Fori(0, N_GATE // WS) as i:
                for k in range(WS):
                    load(B_GATE + k, i, cols(w_in_v, i * 512 + (COL_GATE + 128 * k)))
            for b0, view in ((B_BRD, brd_v), (B_BRA, bra_v)):
                with sp.Fori(0, N_BR // WS) as i:
                    for k in range(WS):
                        load(b0 + k, i, cols(view, i * 512 + 128 * k))
            sp.wait_ge(ya_ok, S // C)
            sp.dma_start(x1[:, :, :], x_v[:, :, :]).then_inc(x_again, 16)
            with sp.Fori(0, N_OUT // WS) as i:
                for k in range(WS):
                    load(B_OUT + k, i, w_out[0, bass.ds(i * 512 + 128 * k, 128), :])
            sp.dma_start(fw, final_norm_w.unsqueeze(0).to_broadcast([P, D])).then_inc(fw_ok, 16)
            with sp.Fori(0, N_UP // WS) as i:
                for k in range(WS):
                    load(B_UP + k, i, cols(up_v, i * 512 + 128 * k))
            with sp.Fori(0, N_DOWN // WS) as i:
                for k in range(WS):
                    load(B_DOWN + k, i, w_mlp_down[0, bass.ds(i * 512 + 128 * k, 128), :])
            for t in range(TT):
                sp.wait_ge(y_fin, t + 1)
                sp.dma_start(out_v[:, t, :], x1[:, t, :]).then_inc(out_sent, 16)
            sp.wait_ge(out_sent, 16 * TT)

        @block.gpsimd
        def _(pool):
            def lo(b, i=0):
                pool.wait_ge(w_hi_ok, b + WS * i + 1)
                pool.tensor_tensor(w_lo[:, b % WS, :], raw[:, b % RS, :], w_hi[:, b % WS, :].bitcast(F32),
                                   ALU.subtract).then_inc(w_ok, 1)

            with pool.Fori(0, N_CONV // WS + 1) as i:
                for k in range(WS):
                    lo(k, i)
            with pool.Fori(0, TT) as t:
                pool.wait_ge(kq_ok, t * 2 + 2)
                pool.wait_ge(eg_ok, t + 1)
                for c in range(2):
                    for s, part in ((0, c), (1, 1 - c)):
                        pool.tensor_tensor(KD[:, :, c, part, :], KQ[:, :, s, C * c:C * c + C],
                                           EG[:, :, C * c:C * c + C], ALU.mult).then_inc(kdq_ok, 1)
                for k in range(WS):
                    lo(B_DN + WS + k, t)
            lo(B_KV + WS)
            lo(B_KV + WS + 1)
            with pool.Fori(0, S // P) as s:
                for c in range(2):
                    pool.wait_ge(rden_ok, s * 2 + (c + 1))
                    pool.tensor_tensor(PR, PR, col(den), ALU.mult).then_inc(pn_ok, 1)
                    lo(B_GATE + WS + 2 * c, s)
                    lo(B_GATE + WS + 2 * c + 1, s)
            with pool.Fori(0, (B_END - B_BRD) // WS - 1) as i:
                for k in range(WS):
                    lo(B_BRD + WS + k, i)

        @block.tensor
        def _(pe):
            def products(out_ap, lhs, rhs, first, last):
                m = None
                for n, (a, b) in enumerate(((0, 0), (0, 1), (1, 0))):
                    m = pe.matmul(out_ap, lhs[a], rhs[b], start=first and n == 0, stop=last and n == 2)
                return m

            def part_f(b, i, k0, k1, tiles=None, free=False):
                f = b if b < B_OUT else b - N_OUT
                if k0 == 0:
                    pe.wait_ge(w_ok, b + WS * i + 1)
                    if f >= 2:
                        pe.wait_ge(blk_read, f + WS * i - 1)
                for k in range(k0, k1):
                    w = [h[:, b % WS, 128 * k:128 * k + 128] for h in (w_hi, w_lo)]
                    if tiles is not None:
                        pe.wait_ge(a_ok, tiles + k + 1)
                    m = products(ps[:, f % 2, :], w, (act_hi[:, k, :], act_lo[:, k, :]), k == 0, k == KT - 1)
                    if free and k < KT - 1:
                        m.then_inc(a_free, 1)
                if k1 == KT:
                    m.then_inc(blk_mm, 1)

            def block_f(b, i=0, tiles=None, free=False):
                part_f(b, i, 0, KT, tiles, free)

            def block_t(b, i, slot, first, last):
                pe.wait_ge(w_ok, b + WS * i + 1)
                for t in range(TT):
                    a = [h[:, slot, 128 * t:128 * t + 128] for h in (act_hi, act_lo)]
                    for n in range(2):
                        w = [h[:, b % WS, 512 * n:512 * n + 512] for h in (w_hi, w_lo)]
                        m = products(ps[:, 2 * t + n, :], a, w, first, last)
                    if last and t < TT - 1:
                        m.then_inc(rows_mm, 1)
                m.then_inc(blk_mm, 1)

            def transposes_in(tiles):
                for t in range(TT):
                    pe.wait_ge(xn_ok, tiles + t + 1)
                    for k in range(KT):
                        m = pe.transpose(ps[:, k, 128 * t:128 * t + 128], xn[:, t, 128 * k:128 * k + 128], const["ident"])
                        if t == TT - 1:
                            m.then_inc(xt_mm, 1)

            pe.wait_ge(consts_in, 16)
            pe.wait_ge(params_in, 4 * 16)
            pe.transpose(ps[:, 0, 0:128], prow, const["ident"]).then_inc(par_mm, 1)
            pe.wait_ge(par_ok, 1)
            transposes_in(0)
            block_f(0, 0, 0)
            pe.wait_ge(wb_ok, 1)
            for k in range(KT):
                w = [wb[:, 2 * NH * k:2 * NH * (k + 1)] for wb in (wb_hi, wb_lo)]
                m = products(ps[0:2 * NH, 2, :], w, (act_hi[:, k, :], act_lo[:, k, :]), k == 0, k == KT - 1)
            m.then_inc(bd_mm, 1)
            block_f(1)
            pe.wait_ge(bd_ok, 1)
            for t in range(TT):
                m = pe.transpose(ps[:, 3, 16 * t:16 * t + 16], bd_rows[:, 128 * t:128 * t + 128], const["ident"][0:16, 0:16])
            m.then_inc(bdt_mm, 1)
            for b in range(2, WS):
                block_f(b)
            with pe.Fori(0, N_CONV // WS - 1) as i:
                for k in range(WS):
                    block_f(WS + k, i)
            pe.wait_ge(g_ok, 1)
            pe.matmul(ps[:, 3, 0:32], const["tri"], dec, start=True, stop=True)
            pe.matmul(ps[:, 4, 0:32], const["later"], dec, start=True, stop=True).then_inc(gc_mm, 1)
            pe.wait_ge(gc_ok, 2)
            pe.wait_ge(s0_ok, 1)

            def quarter(t, j):
                part_f(B_DN + j // 4, t, 2 * (j % 4), 2 * (j % 4) + 2)

            with pe.Fori(0, TT) as t:
                for j in (0, 1, 2):
                    quarter(t, j)
                for n in range(2):
                    pe.wait_ge(sq_ok, t * 2 + (n + 1))
                    for g in range(HALVES):
                        m = pe.matmul(ps[:, 2 + 2 * n + g, :], const["ones"],
                                      (X, T)[n][:, GH * g:GH * g + GH, :], start=True, stop=True)
                    m.then_inc(ss_mm, 1)
                pe.wait_ge(g_now_ok, t + 1)
                for h in range(NH):
                    m = pe.matmul(heads(6)[:, h, :], g_now[:, h:h + 1].to_broadcast([P, 128]), const["tri"],
                                  start=h % GH == 0, stop=True, skip_group_check=True)
                m.then_inc(grow_mm, 1)
                for j in (3, 4, 5):
                    quarter(t, j)
                pe.wait_ge(kq_ok, t * 2 + 2)
                pe.wait_ge(lns_ok, t * 2 + 2)
                for h in range(NH):
                    m = pe.matmul(ps[:, 2 + h // 2, 256 * (h % 2):256 * (h % 2) + 256], KQ[:, h, 0, :],
                                  KQ[:, h, :, :], start=h % 2 == 0, stop=True, skip_group_check=True)
                m.then_inc(gram_mm, 1)
                for j in (6, 7, 8):
                    quarter(t, j)
                pe.wait_ge(vs_ok, t + 1)
                pe.wait_ge(l_raw, t + 1)
                pe.wait_ge(int_ok, t + 1)
                for h in range(NH):
                    m = pe.transpose(heads(2)[:, h, :], VS[:, h, :], const["ident"])
                m.then_inc(vt_mm, 1)
                for h in range(NH):
                    m = pe.transpose(heads(4)[:, h, :], KQ[:, h, 0, :], const["ident"])
                m.then_inc(kt_mm, 1)
                pe.wait_ge(l_ok, t + 1)
                pe.wait_ge(eg_ok, t + 1)
                for h in range(NH):
                    m = pe.transpose(heads(6)[:, h, :], L[:, h, :], const["ident"])
                m.then_inc(lt_mm, 1)
                quarter(t, 9)
                for lv in range(len(LEVELS)):
                    last = lv == len(LEVELS) - 1
                    for g in range(HALVES):
                        if lv == 0:
                            pe.wait_ge(lt_ok, t + 1)
                            pe.wait_ge(x0_ok, t + 1)
                            pe.wait_ge(vtok_ok, t + 1)
                        else:
                            pe.wait_ge(x_upd, t * 8 + (2 * lv - 1 + g))
                        for h in range(GH * g, GH * g + GH):
                            m = pe.matmul(heads(2)[:, h, :], LT[:, h, :], X[:, h, :], start=h % GH == 0, stop=True,
                                          skip_group_check=True)
                        m.then_inc(y_mm, 1)
                    if lv in (1, 3):
                        quarter(t, 10 + lv // 2)
                    for g in range(HALVES):
                        pe.wait_ge(y_ok, t * 10 + (2 * lv + g + 1))
                        if lv == 0:
                            pe.wait_ge(t0_ok, t + 1)
                            pe.wait_ge(kdec_ok, t + 1)
                        else:
                            pe.wait_ge(t_upd, t * 10 + (2 * lv - 1 + g))
                        for h in range(GH * g, GH * g + GH):
                            if last:
                                m = pe.matmul(heads(6)[:, h, :], Y[:, h, :], T[:, h, :], start=h % GH == 0,
                                              stop=True, skip_group_check=True)
                            else:
                                m = pe.matmul(heads(4)[:, h, :], T[:, h, :], Y[:, h, :], start=h % GH == 0,
                                              stop=True, skip_group_check=True)
                        m.then_inc(xt2_mm, 1)
                quarter(t, 12)
                pe.wait_ge(tb_ok, t + 1)
                pe.wait_ge(kdq_ok, t * 4 + 4)
                for c in range(2):
                    p0 = C * c
                    own, other = slice(p0, p0 + C), slice(C - p0, 2 * C - p0)
                    for g in range(HALVES):
                        if c:
                            pe.wait_ge(s_upd, t * 4 + (1 + g))
                            pe.wait_ge(o_ok, t * 4 + (1 + g))
                        for h in range(GH * g, GH * g + GH):
                            m = pe.matmul(heads(2)[:, h, :], KD[:, h, c, :, :].rearrange("p s n -> p (s n)"), ST[:, h, :],
                                          start=h % GH == 0, stop=False, skip_group_check=True)
                        m.then_inc(kq_mm, 1)
                    for g in range(HALVES):
                        pe.wait_ge(r_ok, t * 4 + (2 * c + g + 1))
                        if c:
                            pe.wait_ge(vn_ok, t * 4 + (1 + g))
                        for h in range(GH * g, GH * g + GH):
                            m = pe.matmul(heads(4)[:, h, :], T[own, h, :], R[own, h, :],
                                          start=h % GH == 0, stop=True, skip_group_check=True)
                        m.then_inc(vn_mm, 1)
                    for g in range(HALVES):
                        pe.wait_ge(vn_ok, t * 4 + (2 * c + g + 1))
                        for h in range(GH * g, GH * g + GH):
                            m = pe.matmul(heads(6)[:, h, :], TAILK[own, h, :], VN[own, h, :],
                                          start=h % GH == 0, stop=True, skip_group_check=True)
                        m.then_inc(su_mm, 1)
                        for h in range(GH * g, GH * g + GH):
                            m = pe.matmul(heads(2)[other, h, :], INT[own, h, p0:p0 + C], VN[own, h, :],
                                          start=False, stop=True, skip_group_check=True)
                        m.then_inc(o_mm, 1)
                for j in (13, 14, 15):
                    quarter(t, j)
                pe.wait_ge(on_ok, t + 1)
                for h in range(NH):
                    m = pe.transpose(heads(2)[:, h, :], O[:, h, :], const["ident"])
                m.then_inc(on_mm, 1)
                pe.wait_ge(yd_ok, t * 2 + 2)
                pe.wait_ge(s_upd, t * 4 + 4)

            block_f(B_KV)
            block_f(B_KV + 1)

            def attend(n, c, s, before, last):
                pe.wait_ge(qs_ok, n + 1)
                pe.wait_ge(kvs_ok, n + 1)
                for e in range(2):
                    for r in range(4):
                        m = pe.matmul(ps[:, 2 + e, 128 * r:128 * r + 128],
                                      qs[c][64 * e:64 * e + 64, 2 * r:2 * r + 2, :].rearrange("p a b -> p (a b)"),
                                      kvs[c][64 * e:64 * e + 64, r // 2, :], start=r == 0, stop=True,
                                      skip_group_check=True)
                m.then_inc(sc_mm, 1)
                pe.transpose(ps[:, 7, 0:128], kvs[c][:, 2, :], const["ident"]).then_inc(vw_mm, 1)
                block_f(B_GATE + 2 * c, s)
                second = (B_GATE + 2 * c + 1, s)
                part_f(*second, 0, 4, None, last)
                pe.wait_ge(pn_ok, n + 1)
                for a in range(8):
                    m = pe.transpose(heads(4)[:, a, :], PR[:, a, :], const["ident"])
                m.then_inc(pt_mm, 1)
                part_f(*second, 4, 6, None, last)
                if before:
                    pe.wait_ge(ya_ok, n)
                pe.wait_ge(vw_ok, n + 1)
                pe.wait_ge(pt_ok, n + 1)
                for e in range(2):
                    for j in range(2):
                        m = pe.matmul(ps[64 * e:64 * e + 64, 6, 256 * j:256 * j + 256], vt2[c][:, 64 * j:64 * j + 64],
                                      PT[:, 4 * e + 2 * j:4 * e + 2 * j + 2, :], start=j == 0, stop=True,
                                      skip_group_check=True)
                m.then_inc(pv_mm, 1)
                part_f(*second, 6, 8, None, last)

            attend(0, 0, 0, False, False)
            attend(1, 1, 0, True, False)
            with pe.Fori(1, S // P - 1) as s:
                for c in range(2):
                    attend(s * 2 + c, c, s, True, False)
            attend(6, 0, 3, True, False)
            attend(7, 1, 3, True, True)

            for b0, tiles in ((B_BRD, 8), (B_BRA, 16)):
                for k in range(N_BR):
                    block_f(b0 + k, 0, tiles if k == 0 else None, k == N_BR - 1)
            pe.wait_ge(blk_read, B_OUT)
            for k in range(N_OUT):
                pe.wait_ge(a_ok, 24 + k + 1)
                block_t(B_OUT + k, 0, k, k == 0, k == N_OUT - 1)
            transposes_in(TT)
            block_f(B_UP, 0, 32)
            for k in range(1, WS):
                block_f(B_UP + k)
            with pe.Fori(0, N_UP // WS - 2) as i:
                for k in range(WS):
                    block_f(B_UP + WS + k, i)
            for k in range(WS):
                block_f(B_UP + N_UP - WS + k, 0, None, k == WS - 1)
            pe.wait_ge(blk_read, B_DOWN - N_OUT)

            def down(i, first=False, last=False):
                for k in range(WS):
                    pe.wait_ge(a_ok, i * WS + (40 + k + 1))
                    block_t(B_DOWN + k, i, k, first and k == 0, last and k == WS - 1)

            down(0, first=True)
            with pe.Fori(1, N_DOWN // WS - 1) as i:
                down(i)
            pe.wait_ge(w_ok, B_END)
            pe.wait_ge(a_ok, 40 + N_DOWN)
            for t in range(TT):
                for k in range(WS):
                    b = B_END - WS + k
                    a = [h[:, k, 128 * t:128 * t + 128] for h in (act_hi, act_lo)]
                    for n in range(2):
                        w = [h[:, b % WS, 512 * n:512 * n + 512] for h in (w_hi, w_lo)]
                        m = products(ps[:, 2 * t + n, :], a, w, False, k == WS - 1)
                m.then_inc(rows_mm, 1)

        @block.scalar
        def _(act):
            def hi(b, i=0):
                act.wait_ge(raw_in[b % RS], i * (16 * WS // RS) + 16 * (b // RS + 1))
                if b >= WS:
                    act.wait_ge(blk_mm, i * WS + (b - WS + 1))
                act.activation(w_hi[:, b % WS, :], raw[:, b % RS, :], ACT.Copy).then_inc(w_hi_ok, 1)

            def row_scale(done, t, rows, junk):
                act.activation(junk, rows, ACT.Square, accum_out=ss[:, t:t + 1]).then_inc(ss_ok, 1)
                act.wait_ge(ss_ok, done + t + 1)
                act.activation(rstd[:, t:t + 1], ss[:, t:t + 1], ACT.Ln, bias=eps_c, scale=1.0 / D).then_inc(ln_ok, 1)
                act.wait_ge(ln_ok, done + t + 1)
                act.activation(rstd[:, t:t + 1], rstd[:, t:t + 1], ACT.Exp, scale=-0.5).then_inc(rstd_ok, 1)

            def norm_hi(done, row):
                for k in range(KT):
                    act.wait_ge(xt_mm, done + k + 1)
                    act.activation(act_hi[:, k, :], ps[:, k, :], ACT.Identity,
                                   scale=par[:, row + k:row + k + 1]).then_inc(a_hi_ok, 1)

            act.preload_act_table_set("natural_log_exp_and_others")
            act.wait_ge(eps_ok, 1)
            for t in range(TT):
                act.wait_ge(x_in[t], 16)
                row_scale(0, t, xn[:, t, :], flat(O_JUNK0 + D * t, D))
            hi(0)
            act.wait_ge(par_ok, 1)
            norm_hi(0, PR_MIX)
            hi(1)
            act.wait_ge(wb_in, 16)
            act.activation(wb_hi[:, :], wbeta, ACT.Copy).then_inc(wb_hi_ok, 1)
            hi(2)
            hi(3)
            act.wait_ge(sm, 3)
            act.activation(tmp[1], tmp[1], ACT.Exp).then_inc(sm_act, 1)
            act.activation(beta3, bd_cols[:, :, 0:NH], ACT.Exp, scale=-1.0).then_inc(sm_act, 1)
            act.wait_ge(small_in, 4 * 16)
            act.activation(alog, alog, ACT.Exp).then_inc(sm_act, 1)
            act.wait_ge(sm_act, 1)
            act.activation(tmp[1], tmp[1], ACT.Ln, bias=1.0).then_inc(sm_act, 1)
            with act.Fori(0, N_CONV // WS) as i:
                for k in range(WS):
                    act.wait_ge(blk_read, i * WS + (k + 1))
                    apart(act)
                    q = qkv[:, bass.ds(i * WS + k, 1), :]
                    act.activation(q, q, ACT.Silu).then_inc(conv_ok, 1)
                    hi(WS + k, i)
            act.preload_act_table_set("natural_log_exp_and_others")
            act.wait_ge(gc_mm, 1)
            act.activation(tail, ps[:, 4, 0:32], ACT.Exp).then_inc(gc_ok, 1)
            act.wait_ge(conv_ok, N_CONV)

            def filler(t, k):
                act.wait_ge(blk_mm, t * WS + (B_DN + k + 1))
                apart(act)
                act.activation(qkv[:, 4 * k:4 * k + 4, bass.ds(t * 128, 128)],
                               ps[:, k % 2, :].rearrange("p (a n) -> p a n", a=4), ACT.Copy).then_inc(blk_read, 1)
                hi(B_DN + WS + k, t)

            with act.Fori(0, TT) as t:
                now = bass.ds(t * 128, 128)
                for n in range(2):
                    act.activation((X, T)[n], qkv[:, 8 - 8 * n:16 - 8 * n, now], ACT.Square).then_inc(sq_ok, 1)
                for n in range(2):
                    act.wait_ge(ss_mm, t * 2 + (n + 1))
                    act.activation((X, T)[n], heads(2 + 2 * n), ACT.Ln, bias=eps_c).then_inc(lns_ok, 1)
                act.wait_ge(arg_ok, t + 1)
                act.activation(EG, heads(6), ACT.Exp).then_inc(eg_ok, 1)
                for n in range(2):
                    act.wait_ge(lns_ok, t * 2 + (n + 1))
                    act.activation((X, T)[n], (X, T)[n], ACT.Exp, scale=-0.5,
                                   bias=(zero_c, lnq_c)[n]).then_inc(rn_ok, 1)
                act.activation(VS, qkv[:, 16:24, now], ACT.Copy).then_inc(vs_ok, 1)
                for n in range(2):
                    act.wait_ge(darg_ok, t * 2 + (n + 1))
                    act.activation((L, INT)[n], (L, INT)[n], ACT.Exp).then_inc(dexp_ok, 1)
                act.wait_ge(kq_ok, t * 2 + 2)
                filler(t, 0)
                filler(t, 1)
                act.wait_ge(vt_mm, t + 1)
                act.activation(VTOK, heads(2), ACT.Copy).then_inc(vtok_ok, 1)
                act.wait_ge(lt_mm, t + 1)
                act.activation(LT, heads(6), ACT.Copy).then_inc(lt_ok, 1)
                filler(t, 2)
                for c in range(2):
                    other = slice(C - C * c, 2 * C - C * c)
                    own = slice(C * c, C * c + C)
                    for g in range(HALVES):
                        hs = slice(GH * g, GH * g + GH)
                        act.wait_ge(vn_mm, t * 4 + (2 * c + g + 1))
                        act.activation(VN[own, hs, :], heads(4)[own, hs, :], ACT.Copy).then_inc(vn_ok, 1)
                    for g in range(HALVES):
                        hs = slice(GH * g, GH * g + GH)
                        act.wait_ge(o_mm, t * 4 + (2 * c + g + 1))
                        act.activation(O[other, hs, :], heads(2)[other, hs, :], ACT.Copy).then_inc(o_ok, 1)
                act.wait_ge(oss_ok, t + 1)
                act.activation(ors, oss, ACT.Ln, scale=1.0 / 128, bias=eps_c).then_inc(oln_ok, 1)
                act.wait_ge(oln_ok, t + 1)
                act.activation(ors, ors, ACT.Exp, scale=-0.5).then_inc(ors_ok, 1)
                filler(t, 3)
                act.wait_ge(on_mm, t + 1)
                apart(act)
                for c in range(2):
                    act.activation(yd[:, :, bass.ds(t * 128 + C * c, C)], heads(2)[:, :, C - C * c:2 * C - C * c],
                                   ACT.Identity, scale=dnw).then_inc(yd_ok, 1)

            act.wait_ge(kv_pad, 1)
            act.wait_ge(blk_mm, B_KV + 1)
            for j in range(2):
                for e in range(2):
                    act.activation(kvt[64 * e:64 * e + 64, j, C:], ps[64 * j:64 * j + 64, 0, :],
                                   ACT.Copy).then_inc(kv_ok, 1)
            act.wait_ge(kv_ok, 4)
            act.activation(kvt[0:1, 0, 0:1], kvt[0:1, 0, 0:1], ACT.Copy).then_inc(blk_read, 1)
            hi(B_KV + WS)
            act.wait_ge(blk_mm, B_KV + 2)
            act.activation(kvt[:, 2, C:], ps[:, 1, :], ACT.Copy).then_inc(blk_read, 1)
            hi(B_KV + WS + 1)
            act.wait_ge(yd_ok, 2 * TT)
            for j in range(2):
                act.activation(qkv[:, 4 * j:4 * j + 4, :], qkv[:, 4 * j:4 * j + 4, :], ACT.Silu).then_inc(dz_ok, 1)
            act.preload_act_table_set("exp_and_others")
            act.wait_ge(blk_read, B_KV + 2)

            queries = arena[:, QKV:QKV + 24 * S].rearrange("p (b s t u q) -> p b s t u q", b=6, s=4, t=4, u=2)

            def stage(n, c, s):
                act.activation(qs[c].rearrange("p (t j) q -> p j t q", j=2),
                               queries[:, 2:4, bass.ds(s, 1), :, c, :].rearrange("p b s t q -> p b (s t) q"),
                               ACT.Copy).then_inc(qs_ok, 1)
                act.activation(kvs[c], kvt[:, :, bass.ds(n * C, 128)], ACT.Copy).then_inc(kvs_ok, 1)

            def attend(n, c, s, last=False):
                act.wait_ge(vw_mm, n + 1)
                act.activation(vt2[c], ps[:, 7, 0:128], ACT.Copy).then_inc(vw_ok, 1)
                act.wait_ge(pe_ok, n + 1)
                act.activation(PR, PR, ACT.Exp).then_inc(exp_ok, 1)
                act.wait_ge(esd_ok, n + 1)
                act.activation(es, es, ACT.Exp).then_inc(es_ok, 1)
                if not last:
                    stage(n + 1, 1 - c, s + c)
                hi(B_GATE + WS + 2 * c, s)
                if last:
                    act.wait_ge(ydz_ok, 4)
                    for k in range(KT):
                        act.wait_ge(a_free, k + 1) if k < KT - 1 else act.wait_ge(blk_mm, B_BRD)
                        act.activation(act_hi[:, k, :], yd[:, k, :], ACT.Copy).then_inc(a_hi_ok, 1)
                act.wait_ge(pv_mm, n + 1)
                apart(act)
                act.activation(yatt[:, :, bass.ds(n * C, C)], ps[:, 6, :].rearrange("p (h q) -> p h q", h=KT),
                               ACT.Copy).then_inc(ya_ok, 1)
                hi(B_GATE + WS + 2 * c + 1, s)

            stage(0, 0, 0)
            with act.Fori(0, S // P - 1) as s:
                for c in range(2):
                    attend(s * 2 + c, c, s)
            attend(6, 0, 3)
            attend(7, 1, 3, True)

            act.wait_ge(blk_read, B_BRD)
            act.activation(gates[:, 8:16, :], gates[:, 8:16, :], ACT.Sigmoid).then_inc(sig_ok, 1)
            hi(B_BRD + WS)
            act.activation(gates[:, 0:8, :], gates[:, 0:8, :], ACT.Sigmoid).then_inc(sig_ok, 1)
            for k in range(1, N_BR - 1):
                hi(B_BRD + WS + k)
            act.wait_ge(ya_ok, S // C)
            for k in range(KT):
                act.wait_ge(a_free, 7 + k + 1) if k < KT - 1 else act.wait_ge(blk_mm, B_BRA)
                act.activation(act_hi[:, k, :], yatt[:, k, :], ACT.Copy).then_inc(a_hi_ok, 1)
            for k in range(N_BR - 1, 2 * N_BR - 1):
                hi(B_BRD + WS + k)
            for k in range(KT):
                act.wait_ge(a_free, 14 + k + 1) if k < KT - 1 else act.wait_ge(blk_mm, B_OUT)
                act.wait_ge(mg_ok, k + 1)
                act.activation(act_hi[:, k, :], gates[:, k, :], ACT.Copy).then_inc(a_hi_ok, 1)
            for k in range(2 * N_BR - 1, 2 * N_BR + N_OUT):
                hi(B_BRD + WS + k)
            act.preload_act_table_set("natural_log_exp_and_others")
            for t in range(TT):
                act.wait_ge(x1_ok, t + 1)
                row_scale(TT, t, x1[:, t, :], flat(O_JUNK1 + D * t, D))
            norm_hi(KT, PR_MLP)
            with act.Fori(0, N_UP // WS) as i:
                for k in range(WS):
                    act.wait_ge(blk_mm, i * WS + (B_UP + k + 1))
                    apart(act)
                    act.activation(a_t[:, bass.ds(i * WS + k, 1), :].rearrange("p a n -> p (a n)"), ps[:, k % 2, :],
                                   ACT.Relu).then_inc(relu_ok, 1)
                    hi(B_UP + WS + k, i)

            def squares_hi(k, i=0):
                act.wait_ge(blk_read, i * WS + (B_UP - N_OUT + k + 1))
                if k < WS:
                    act.wait_ge(a_free, 21 + k + 1)
                else:
                    act.wait_ge(blk_mm, i * WS + (B_DOWN + k - WS + 1))
                apart(act)
                act.activation(act_hi[:, k % WS, :], a_t[:, bass.ds(i * WS + k, 1), :].rearrange("p a n -> p (a n)"),
                               ACT.Copy).then_inc(a_hi_ok, 1)

            for k in range(WS):
                squares_hi(k)
            with act.Fori(0, N_DOWN // WS - 1) as i:
                for k in range(WS):
                    hi(B_DOWN + WS + k, i)
                    squares_hi(WS + k, i)
            for t in range(TT):
                act.wait_ge(y_add, t + 1)
                row_scale(2 * TT, t, x1[:, t, :], flat(O_JUNK1 + D * t, D))

        @block.vector
        def _(dve):
            def norm_lo(done, row):
                for k in range(KT):
                    dve.wait_ge(a_hi_ok, done + k + 1)
                    dve.scalar_tensor_tensor(out=act_lo[:, k, :], in0=ps[:, k, :], scalar=par[:, row + k:row + k + 1],
                                             in1=act_hi[:, k, :].bitcast(F32), op0=ALU.mult,
                                             op1=ALU.subtract).then_inc(a_ok, 1)

            def split_lo(done, src):
                for k in range(KT):
                    dve.wait_ge(a_hi_ok, done + k + 1)
                    dve.tensor_tensor(act_lo[:, k, :], src[:, k, :], act_hi[:, k, :].bitcast(F32),
                                      ALU.subtract).then_inc(a_ok, 1)

            dve.memset(eps_c, EPS)
            dve.memset(zero_c, 0.0)
            dve.memset(lnq_c, LN_Q_SCALE).then_inc(eps_ok, 1)
            dve.wait_ge(par_mm, 1)
            dve.tensor_copy(par, ps[:, 0, 0:128]).then_inc(par_ok, 1)
            for t in range(TT):
                dve.wait_ge(rstd_ok, t + 1)
                dve.tensor_scalar(xn[:, t, :], xn[:, t, :], rstd[:, t:t + 1], None, ALU.mult).then_inc(xn_ok, 1)
            dve.wait_ge(par_ok, 1)
            norm_lo(0, PR_MIX)
            dve.wait_ge(wb_hi_ok, 1)
            dve.tensor_tensor(wb_lo[:, :], wbeta, wb_hi[:, :].bitcast(F32), ALU.subtract).then_inc(wb_ok, 1)
            dve.wait_ge(bd_mm, 1)
            dve.tensor_copy(bd_rows, ps[0:2 * NH, 2, :]).then_inc(bd_ok, 1)
            dve.wait_ge(bdt_mm, 1)
            dve.wait_ge(small_in, 4 * 16)
            y3, z3 = (a.rearrange("p (t h) -> p t h", h=NH) for a in tmp)

            def rows(a):
                return a.unsqueeze(1).to_broadcast([P, TT, NH])

            dve.tensor_tensor(y3, bd_cols[:, :, NH:2 * NH], rows(dtb), ALU.add).then_inc(sm, 1)
            dve.wait_ge(sm, 1)
            dve.tensor_scalar(tmp[1], tmp[0], -1.0, None, ALU.mult).then_inc(sm, 1)
            dve.wait_ge(sm, 2)
            dve.tensor_tensor(tmp[1], tmp[0], tmp[1], ALU.min).then_inc(sm, 1)
            dve.wait_ge(sm_act, 4)
            dve.wait_ge(sm, 3)
            dve.scalar_tensor_tensor(out=tmp[0], in0=tmp[0], scalar=0.0, in1=tmp[1], op0=ALU.max,
                                     op1=ALU.add).then_inc(sm, 1)
            dve.tensor_scalar(beta, beta, 1.0, None, ALU.add).then_inc(sm, 1)
            dve.wait_ge(sm, 5)
            dve.scalar_tensor_tensor(out=dec3, in0=y3, scalar=-1.0, in1=rows(alog), op0=ALU.mult,
                                     op1=ALU.mult).then_inc(g_ok, 1)
            dve.reciprocal(beta, beta).then_inc(sm, 1)
            for hl in range(2):
                rs = slice(64 * hl, 64 * hl + 64)
                dve.tensor_copy(sinks[rs, :].rearrange("p (e r) -> p e r", e=2),
                                sinks_all[rs, :].rearrange("p (r l e) -> p l e r", l=2, e=2)[:, hl]).then_inc(sink_ok, 1)
            with dve.Fori(0, N_CONV // WS) as i:
                for k in range(WS):
                    dve.wait_ge(blk_mm, i * WS + (k + 1))
                    q = qkv[:, bass.ds(i * WS + k, 1), :].rearrange("p a n -> p (a n)")
                    z = ps[:, k % 2, :]
                    taps = [par[:, bass.ds(i * WS + (PR_CONV + 24 * j + k), 1)] for j in range(4)]
                    dve.tensor_scalar(q, z, taps[3], None, ALU.mult).then_inc(conv_tap, 1)
                    for j in (2, 1, 0):
                        d = 3 - j
                        dve.wait_ge(conv_tap, i * (3 * WS) + (3 * k + d))
                        m = dve.scalar_tensor_tensor(out=q[:, d:S], in0=z[:, 0:S - d], scalar=taps[j],
                                                     in1=q[:, d:S], op0=ALU.mult, op1=ALU.add)
                        m.then_inc(conv_tap if j else blk_read, 1)
            dve.memset(arena[:, O_S:O_S + 1024], 0.0).then_inc(s0_ok, 1)
            dve.wait_ge(gc_mm, 1)
            dve.tensor_copy(gcol, ps[:, 3, 0:32]).then_inc(gc_ok, 1)
            dve.wait_ge(sm, 6)
            dve.wait_ge(gc_ok, 2)

            with dve.Fori(0, TT) as t:
                now = bass.ds(t * 128, 128)

                def token_col(a3):
                    return col(a3[:, bass.ds(t, 1), :].rearrange("p a h -> p (a h)"))

                dve.tensor_copy(g_now, dec3[:, bass.ds(t, 1), :].rearrange("p a h -> p (a h)")).then_inc(g_now_ok, 1)
                dve.wait_ge(grow_mm, t + 1)
                dve.tensor_tensor(INT, heads(6), token_col(gcol3), ALU.subtract).then_inc(arg_ok, 1)
                dve.wait_ge(arg_ok, t + 1)
                dve.tensor_tensor(L, mat("mask_l"), INT, ALU.subtract).then_inc(darg_ok, 1)
                dve.tensor_tensor(INT, mat("mask_t"), INT, ALU.add).then_inc(darg_ok, 1)
                dve.wait_ge(eg_ok, t + 1)
                dve.tensor_copy(gl3, EG[:, :, C - 1:2 * C:C]).then_inc(gl_ok, 1)
                for n in range(2):
                    dve.wait_ge(rn_ok, t * 2 + (n + 1))
                    dve.tensor_tensor(KQ[:, :, n, :], qkv[:, 8 - 8 * n:16 - 8 * n, now], (X, T)[n],
                                      ALU.mult).then_inc(kq_ok, 1)
                grams = ps[:, 2:6, :].rearrange("p b (h s n) -> p (b h) s n", h=2, s=2)
                dve.wait_ge(gram_mm, t + 1)
                dve.wait_ge(dexp_ok, t * 2 + 1)
                dve.tensor_tensor(L, grams[:, :, 0, :], L, ALU.mult).then_inc(l_raw, 1)
                dve.wait_ge(dexp_ok, t * 2 + 2)
                dve.tensor_tensor(INT, grams[:, :, 1, :], INT, ALU.mult).then_inc(int_ok, 1)
                dve.wait_ge(l_raw, t + 1)
                dve.tensor_tensor(L, L, token_col(beta3), ALU.mult).then_inc(l_ok, 1)
                dve.wait_ge(l_ok, t + 1)
                dve.tensor_tensor(Y, L, mat("m1"), ALU.mult).then_inc(y1_ok, 1)
                dve.wait_ge(y1_ok, t + 1)
                dve.tensor_tensor(X, mat("ident"), Y, ALU.subtract).then_inc(x0_ok, 1)
                dve.wait_ge(x0_ok, t + 1)
                dve.transpose(T, X).then_inc(t0_ok, 1)
                dve.wait_ge(kt_mm, t + 1)
                dve.wait_ge(lt_mm, t + 1)
                dve.tensor_tensor(TAILK, heads(4), token_col(tail3), ALU.mult).then_inc(kdec_ok, 1)
                for lv, name in enumerate(LEVELS):
                    for g in range(HALVES):
                        hs = slice(GH * g, GH * g + GH)
                        dve.wait_ge(y_mm, t * 10 + (2 * lv + g + 1))
                        dve.tensor_tensor(Y[:, hs, :], heads(2)[:, hs, :], mat(name, GH), ALU.mult).then_inc(y_ok, 1)
                    for g in range(HALVES):
                        hs = slice(GH * g, GH * g + GH)
                        dve.wait_ge(xt2_mm, t * 10 + (2 * lv + g + 1))
                        if lv < len(LEVELS) - 1:
                            dve.tensor_tensor(X[:, hs, :], X[:, hs, :], heads(4)[:, hs, :], ALU.subtract).then_inc(x_upd, 1)
                            dve.wait_ge(x_upd, t * 8 + (2 * lv + g + 1))
                            dve.transpose(T[:, hs, :], X[:, hs, :]).then_inc(t_upd, 1)
                        else:
                            dve.tensor_tensor(T[:, hs, :], T[:, hs, :], heads(6)[:, hs, :], ALU.subtract).then_inc(t_upd, 1)
                dve.wait_ge(t_upd, t * 10 + 10)
                dve.tensor_tensor(T, T, token_col(beta3), ALU.mult).then_inc(tb_ok, 1)
                for c in range(2):
                    own = slice(C * c, C * c + C)
                    for g in range(HALVES):
                        hs = slice(GH * g, GH * g + GH)
                        dve.wait_ge(kq_mm, t * 4 + (2 * c + g + 1))
                        dve.wait_ge(vtok_ok, t + 1)
                        dve.tensor_tensor(R[own, hs, :], VTOK[own, hs, :], heads(2)[own, hs, :],
                                          ALU.subtract).then_inc(r_ok, 1)
                    for g in range(HALVES):
                        dve.wait_ge(su_mm, t * 4 + (2 * c + g + 1))
                        dve.wait_ge(gl_ok, t + 1)
                        for h in range(GH * g, GH * g + GH):
                            m = dve.scalar_tensor_tensor(out=ST[:, h, :], in0=ST[:, h, :], scalar=gl3[:, h, c:c + 1],
                                                         in1=heads(6)[:, h, :], op0=ALU.mult, op1=ALU.add)
                        m.then_inc(s_upd, 1)
                dve.wait_ge(o_ok, t * 4 + 4)
                dve.tensor_tensor(Y, O, O, ALU.mult).then_inc(osq_ok, 1)
                dve.wait_ge(osq_ok, t + 1)
                dve.tensor_reduce(oss, Y, AX_X, ALU.add).then_inc(oss_ok, 1)
                dve.wait_ge(ors_ok, t + 1)
                dve.tensor_tensor(O, O, col(ors), ALU.mult).then_inc(on_ok, 1)

            dve.memset(kvt[:, :, 0:C], 0.0).then_inc(kv_pad, 1)
            for j in range(2):
                dve.wait_ge(dz_ok, j + 1)
                dve.wait_ge(yd_ok, 2 * TT)
                for half in range(2):
                    y = arena[:, YD:YD + NH * S].rearrange("p (t j s n) -> p t j s n", t=4, j=2, s=4)[:, :, j, 2 * half:2 * half + 2, :]
                    z = arena[:, QKV + 4 * j * S:QKV + 4 * (j + 1) * S].rearrange("p (s t n) -> p t s n", s=4, t=4)[:, :, 2 * half:2 * half + 2, :]
                    dve.tensor_tensor(y, y, z, ALU.mult).then_inc(ydz_ok, 1)

            def attend(n, c, s, first):
                k0 = C if first else 0
                sc = heads(2)[:, :, k0:]
                prk = PR[:, :, k0:]
                w = 128 - k0
                dve.wait_ge(sc_mm, n + 1)
                dve.tensor_reduce(mx, sc, AX_X, ALU.max).then_inc(mx_ok, 1)
                dve.wait_ge(mx_ok, n + 1)
                dve.scalar_tensor_tensor(out=mx, in0=mx, scalar=HD ** -0.5, in1=sinks, op0=ALU.mult,
                                         op1=ALU.max).then_inc(m_ok, 1)
                dve.wait_ge(m_ok, n + 1)
                dve.scalar_tensor_tensor(out=prk, in0=sc, scalar=HD ** -0.5,
                                         in1=mx.unsqueeze(2).to_broadcast([P, 8, w]), op0=ALU.mult,
                                         op1=ALU.subtract).then_inc(pe_ok, 1)
                dve.tensor_tensor(es, sinks, mx, ALU.subtract).then_inc(esd_ok, 1)
                dve.wait_ge(exp_ok, n + 1)
                if first:
                    dve.memset(PR[:, :, 0:C], 0.0)
                dve.tensor_reduce(den, prk, AX_X, ALU.add).then_inc(den_ok, 1)
                dve.wait_ge(es_ok, n + 1)
                dve.wait_ge(den_ok, n * 2 + 1)
                dve.tensor_tensor(den, den, es, ALU.add).then_inc(den_ok, 1)
                dve.wait_ge(den_ok, n * 2 + 2)
                dve.reciprocal(den, den).then_inc(rden_ok, 1)
                for k in range(2):
                    if k:
                        dve.wait_ge(pt_mm, n + 1)
                        dve.tensor_copy(PT, heads(4)).then_inc(pt_ok, 1)
                    dve.wait_ge(blk_mm, s * WS + (B_GATE + 2 * c + k + 1))
                    dve.tensor_scalar(gates[:, bass.ds(s * WS + (2 * c + k), 1), :].rearrange("p a n -> p (a n)"),
                                      ps[:, k, :], par[:, bass.ds(s * WS + (PR_GATE + 2 * c + k), 1)], None,
                                      ALU.add).then_inc(blk_read, 1)

            dve.wait_ge(sink_ok, 2)
            attend(0, 0, 0, True)
            attend(1, 1, 0, False)
            with dve.Fori(1, S // P) as s:
                for c in range(2):
                    attend(s * 2 + c, c, s, False)

            split_lo(8, yd)
            dve.wait_ge(sig_ok, 1)
            for k in range(N_BR):
                dve.wait_ge(blk_mm, B_BRD + k + 1)
                dve.tensor_tensor(gates[:, 8 + k, :], gates[:, 8 + k, :], ps[:, k % 2, :], ALU.mult).then_inc(blk_read, 1)
            dve.wait_ge(ya_ok, S // C)
            split_lo(16, yatt)
            dve.wait_ge(sig_ok, 2)
            for k in range(N_BR):
                dve.wait_ge(blk_mm, B_BRA + k + 1)
                dve.tensor_tensor(gates[:, k, :], gates[:, k, :], ps[:, k % 2, :], ALU.mult).then_inc(blk_read, 1)
                dve.wait_ge(blk_read, B_BRA + k + 1)
                dve.tensor_tensor(gates[:, k, :], gates[:, k, :], gates[:, 8 + k, :], ALU.add).then_inc(mg_ok, 1)
            split_lo(24, gates)
            dve.wait_ge(x_again, 16)
            for t in range(TT):
                dve.wait_ge(rows_mm, t + 1) if t < TT - 1 else dve.wait_ge(blk_mm, B_UP)
                dve.tensor_tensor(x1[:, t, :], x1[:, t, :], ps[:, 2 * t:2 * t + 2, :].rearrange("p b n -> p (b n)"),
                                  ALU.add).then_inc(x1_ok, 1)
            for t in range(TT):
                dve.wait_ge(rstd_ok, TT + t + 1)
                dve.tensor_scalar(xn[:, t, :], x1[:, t, :], rstd[:, t:t + 1], None, ALU.mult).then_inc(xn_ok, 1)
            norm_lo(32, PR_MLP)
            with dve.Fori(0, N_UP // WS) as i:
                for k in range(WS):
                    dve.wait_ge(relu_ok, i * WS + (k + 1))
                    a = a_t[:, bass.ds(i * WS + k, 1), :].rearrange("p a n -> p (a n)")
                    dve.tensor_tensor(a, a, ps[:, k % 2, :], ALU.mult).then_inc(blk_read, 1)
            with dve.Fori(0, N_DOWN // WS) as i:
                for k in range(WS):
                    dve.wait_ge(a_hi_ok, i * WS + (40 + k + 1))
                    dve.tensor_tensor(act_lo[:, k, :], a_t[:, bass.ds(i * WS + k, 1), :].rearrange("p a n -> p (a n)"),
                                      act_hi[:, k, :].bitcast(F32), ALU.subtract).then_inc(a_ok, 1)
            dve.wait_ge(fw_ok, 16)
            for t in range(TT):
                dve.wait_ge(rows_mm, TT - 1 + t + 1)
                dve.tensor_tensor(x1[:, t, :], x1[:, t, :], ps[:, 2 * t:2 * t + 2, :].rearrange("p b n -> p (b n)"),
                                  ALU.add).then_inc(y_add, 1)
                dve.wait_ge(rstd_ok, 2 * TT + t + 1)
                dve.scalar_tensor_tensor(out=x1[:, t, :], in0=x1[:, t, :], scalar=rstd[:, t:t + 1], in1=fw,
                                         op0=ALU.mult, op1=ALU.mult).then_inc(y_fin, 1)


INPUTS = ["x", "norm_mix_w", "w_in", "b_gate", "attn_sinks", "conv_w", "a_log", "dt_bias", "dn_norm_w",
          "w_branch_attn", "w_branch_delta", "w_out", "norm_mlp_w", "w_mlp_up", "w_mlp_down", "final_norm_w"]


def shape_constants(np):
    i, j = np.arange(P)[:, None], np.arange(P)[None, :]
    same = i // C == j // C
    level = {b: (i // (2 * b) == j // (2 * b)) & (i % (2 * b) >= b) & (j % (2 * b) < b) for b in (1, 2, 4, 8, 16, 32)}
    mats = {"ident": i == j, "ones": np.ones((P, P)), "tri": same & (i <= j), "later": same & (i > j),
            "mask_t": np.where(same & (j >= i), 0.0, NEG), "mask_l": np.where(same & (i > j), 0.0, NEG),
            "m1": level[1], **{f"m{b}": level[b] for b in (2, 4, 8, 16, 32)}}
    return np.ascontiguousarray(np.stack([mats[n] for n in CONSTS], axis=1).astype(np.float32))


def kernel(**inputs):
    import numpy as np
    import concourse.bacc as bacc
    from concourse.bass_utils import run_bass_kernel_spmd

    nc = bacc.Bacc("TRN2", target_bir_lowering=False, num_devices=1)
    arrays = {f"in_{n}": np.ascontiguousarray(inputs[n]) for n in INPUTS}
    arrays["in_shape_consts"] = shape_constants(np)
    args = [nc.dram_tensor(n, a.shape, mybir.dt.from_np(a.dtype), kind="ExternalInput").ap() for n, a in arrays.items()]
    args.append(nc.dram_tensor("out_0", (1, S, D), F32, kind="ExternalOutput").ap())
    build(nc, *args)
    return run_bass_kernel_spmd(nc, [arrays], core_ids=[0]).results[0]["out_0"]
```

```python
import math
from contextlib import ExitStack

import concourse.bass as bass
from concourse import mybir
from concourse.alu_op_type import AluOpType as ALU

F32 = mybir.dt.float32
F32R = mybir.dt.float32r
ACT = mybir.ActivationFunctionType
AX_X = mybir.AxisListType.X

P = 128
D = 1024
S = 512
KT = D // P
TT = S // P
C = 64
HD = 64
NH = 8
FF = 4096
EPS = 1e-6
LN_Q_SCALE = -0.5 * math.log(128)
NEG = -1e30
HALVES = 2
T_DELTA, T_ATT, T_MERGED, T_MLP, T_SQ = KT, 2 * KT, 3 * KT, 4 * KT, 5 * KT
GH = NH // HALVES

COL_Q, COL_K, COL_V, COL_CONV = 0, 1024, 1152, 1280
COL_BETA = COL_CONV + 3 * D
COL_DZ = COL_BETA + 2 * NH
COL_GATE = COL_DZ + D

N_CONV, N_DN, N_KV, N_GATE, N_BR, N_OUT, N_UP, N_DOWN = 24, 16, 2, 16, 8, 8, 32, 32
B_CONV = 0
B_DN = B_CONV + N_CONV
B_KV = B_DN + N_DN
B_GATE = B_KV + N_KV
B_BRD = B_GATE + N_GATE
B_BRA = B_BRD + N_BR
B_OUT = B_BRA + N_BR
B_UP = B_OUT + N_OUT
B_DOWN = B_UP + N_UP
B_END = B_DOWN + N_DOWN
WS = 4
RS = 2
LAST = 3

PR_CONV, PR_MIX, PR_GATE, PR_MLP = 0, 96, 104, 120

CONSTS = ["ident", "ones", "tri", "later", "mask_t", "mask_l", "m1", "m2", "m4", "m8", "m16", "m32"]
LEVELS = ["m2", "m4", "m8", "m16", "m32"]

QKV = 0
YD = 24 * S
W0 = YD + 8 * S
(O_KQ, O_KD, O_X, O_T, O_Y, O_TAILK, O_INT, O_L, O_VTOK, O_R, O_VN, O_S, O_O, O_END) = (
    W0 + 1024 * k for k in (0, 2, 4, 5, 6, 7, 8, 9, 10, 11, 12, 13, 14, 15))
O_GATES = W0
O_P, O_PT, O_QS = W0 + 8192, W0 + 9216, W0 + 10240
O_KVS, O_KVT, O_VT2 = W0 + 11264, W0 + 12032, W0 + 13760
O_YATT = QKV + 16 * S
O_XN, O_PROW, O_JUNK0 = W0, W0 + 5120, W0 + 6144
O_X1, O_FW, O_JUNK1 = W0 + 8192, W0 + 12288, W0 + 4096
O_CONST = O_END
O_PT_PAR = O_CONST + 128 * len(CONSTS)
O_SMALL = O_PT_PAR + 128
ARENA = O_SMALL + 512


def build(nc, x, norm_mix_w, w_in, b_gate, attn_sinks, conv_w, a_log, dt_bias, dn_norm_w,
          w_branch_attn, w_branch_delta, w_out, norm_mlp_w, w_mlp_up, w_mlp_down, final_norm_w,
          shape_consts, out):
    w_in_v = w_in[0].rearrange("(k p) n -> p k n", p=P)
    bra_v = w_branch_attn[0].rearrange("(k p) n -> p k n", p=P)
    brd_v = w_branch_delta[0].rearrange("(k p) n -> p k n", p=P)
    up_v = w_mlp_up[0].rearrange("(k p) n -> p k n", p=P)
    x_v = x[0].rearrange("(t p) n -> p t n", p=P)
    out_v = out[0].rearrange("(t p) n -> p t n", p=P)

    with ExitStack() as ctx:
        def sem(name):
            return ctx.enter_context(nc.semaphore(name))

        arena = ctx.enter_context(nc.sbuf_tensor("arena", [P, ARENA], F32))
        raw = ctx.enter_context(nc.sbuf_tensor("raw", [P, RS, D], F32))
        w_hi = ctx.enter_context(nc.sbuf_tensor("w_hi", [P, WS, D], F32R))
        w_lo = ctx.enter_context(nc.sbuf_tensor("w_lo", [P, WS, D], F32R))
        act_hi = ctx.enter_context(nc.sbuf_tensor("act_hi", [P, KT, S], F32R))
        act_lo = ctx.enter_context(nc.sbuf_tensor("act_lo", [P, KT, S], F32R))
        wb_hi = ctx.enter_context(nc.sbuf_tensor("wb_hi", [P, KT * 2 * NH], F32R))
        wb_lo = ctx.enter_context(nc.sbuf_tensor("wb_lo", [P, KT * 2 * NH], F32R))
        ps = ctx.enter_context(nc.psum_tensor("ps", [P, 8, 512], F32))

        def flat(off, n):
            return arena[:, off:off + n]

        def grid(off, a, b):
            return arena[:, off:off + a * b].rearrange("p (a b) -> p a b", a=a)

        def heads(bank):
            return ps[:, bank:bank + 2, :].rearrange("p b (h n) -> p (b h) n", n=128)

        qkv = grid(QKV, 24, S)
        yd = grid(YD, NH, S)
        KQ = arena[:, O_KQ:O_KQ + 2048].rearrange("p (h s n) -> p h s n", h=NH, s=2)
        KD = arena[:, O_KD:O_KD + 2048].rearrange("p (h c s n) -> p h c s n", h=NH, c=2, s=2)
        X, T, Y, TAILK, INT, L, VTOK, R, VN, ST, O = (
            grid(o, NH, 128) for o in (O_X, O_T, O_Y, O_TAILK, O_INT, O_L, O_VTOK, O_R, O_VN, O_S, O_O))
        EG, VS = R, VN
        gates = grid(O_GATES, 16, S)
        PR, PT = grid(O_P, 8, 128), grid(O_PT, 8, 128)
        qs = [grid(O_QS + 512 * c, 8, C) for c in range(2)]
        kvs = [grid(O_KVS + 384 * c, 3, 128) for c in range(2)]
        kvt = grid(O_KVT, 3, S + C)
        vt2 = [flat(O_VT2 + 128 * c, 128) for c in range(2)]
        yatt = grid(O_YATT, KT, S)
        xn = grid(O_XN, TT, D)
        x1 = grid(O_X1, TT, D)
        fw = flat(O_FW, D)
        a_t = grid(0, N_UP, S)
        const = {n: flat(O_CONST + 128 * i, 128) for i, n in enumerate(CONSTS)}
        par = flat(O_PT_PAR, 128)

        at = [O_SMALL]

        def small(n):
            at[0] += n
            assert at[0] <= ARENA
            return flat(at[0] - n, n)

        ss, rstd = small(4), small(4)
        beta, dec, gcol, tail = small(32), small(32), small(32), small(32)
        alog, dtb = small(8), small(8)
        sinks, sinks_all = small(8), small(16)
        dnw = small(1)
        wbeta = small(KT * 2 * NH)
        g_now = small(8)
        gl = small(16)
        oss, ors = small(8), small(8)
        mx, es, den = small(8), small(8), small(8)
        tmp = [small(32), small(32)]
        eps_c, lnq_c, zero_c = small(1), small(1), small(1)
        ms_half = small(1)
        beta3, dec3, gcol3, tail3 = (a.rearrange("p (t h) -> p t h", h=NH) for a in (beta, dec, gcol, tail))
        gl3 = gl.rearrange("p (h c) -> p h c", c=2)
        bd_cols = ps[:, 3, 0:TT * 2 * NH].rearrange("p (t n) -> p t n", t=TT)
        prow = flat(O_PROW, 128)
        bd_rows = arena[0:2 * NH, YD:YD + S]

        def mat(name, n=NH):
            return const[name].unsqueeze(1).to_broadcast([P, n, 128])

        def col(a, n=NH):
            return a.unsqueeze(2).to_broadcast([a.shape[0], n, 128])

        x_in = [sem(f"x_in{t}") for t in range(TT)]
        ident_in, consts_in, params_in, small_in, wb_in, x_again, out_sent = map(
            sem, ["ident_in", "consts_in", "params_in", "small_in", "wb_in", "x_again", "out_sent"])
        raw_in = [sem(f"raw_in{i}") for i in range(RS)]
        w_hi_ok, w_ok, blk_mm, blk_read = map(sem, ["w_hi_ok", "w_ok", "blk_mm", "blk_read"])
        a_hi_ok, a_ok, a_free = sem("a_hi_ok"), sem("a_ok"), sem("a_free")
        par_mm, par_ok, ss_ok, ln_ok, rstd_ok, xn_ok, xt_mm = map(
            sem, ["par_mm", "par_ok", "ss_ok", "ln_ok", "rstd_ok", "xn_ok", "xt_mm"])
        wb_hi_ok, wb_ok, bd_mm, bd_ok, bdt_mm, sm, sm_act, g_ok, gc_mm, gc_ok = map(
            sem, ["wb_hi_ok", "wb_ok", "bd_mm", "bd_ok", "bdt_mm", "sm", "sm_act", "g_ok", "gc_mm", "gc_ok"])
        conv_tap, conv_ok, eps_ok, sink_ok = sem("conv_tap"), sem("conv_ok"), sem("eps_ok"), sem("sink_ok")
        (sq_ok, ss_mm, lns_ok, rn_ok, g_now_ok, grow_mm, eg_ok, gl_ok, kq_ok, arg_ok, darg_ok, dexp_ok, gram_mm,
         l_raw, l_ok, int_ok, vs_ok, vt_mm, kt_mm, vtok_ok, y1_ok, x0_ok, t0_ok, kdec_ok,
         y_mm, y_ok, xt2_mm, x_upd, t_upd, tb_ok, kdq_ok, kq_mm, r_ok, vn_mm, vn_ok, o_mm, su_mm, s_upd, o_ok,
         osq_ok, oss_ok, oln_ok, ors_ok, on_ok, on_mm, yd_ok, s0_ok) = map(sem, [
            "sq_ok", "ss_mm", "lns_ok", "rn_ok", "g_now_ok", "grow_mm", "eg_ok", "gl_ok", "kq_ok", "arg_ok",
            "darg_ok", "dexp_ok", "gram_mm", "l_raw", "l_ok", "int_ok", "vs_ok", "vt_mm", "kt_mm",
            "vtok_ok", "y1_ok", "x0_ok", "t0_ok", "kdec_ok", "y_mm", "y_ok", "xt2_mm",
            "x_upd", "t_upd", "tb_ok", "kdq_ok", "kq_mm", "r_ok", "vn_mm", "vn_ok", "o_mm", "su_mm", "s_upd",
            "o_ok", "osq_ok", "oss_ok", "oln_ok", "ors_ok", "on_ok", "on_mm", "yd_ok", "s0_ok"])
        (dz_ok, ydz_ok, kv_pad, qs_ok, ks_ok, vals_ok, sc_mm, vw_mm, vw_ok, mx_ok, m_ok, pe_ok, esd_ok, exp_ok,
         es_ok, den_ok, rden_ok, pn_ok, pt_mm, pt_ok, pv_mm, ya_ok) = map(sem, [
            "dz_ok", "ydz_ok", "kv_pad", "qs_ok", "ks_ok", "vals_ok", "sc_mm", "vw_mm", "vw_ok", "mx_ok", "m_ok",
            "pe_ok", "esd_ok", "exp_ok", "es_ok", "den_ok", "rden_ok", "pn_ok", "pt_mm", "pt_ok", "pv_mm", "ya_ok"])
        sig_ok, relu_ok, mg_ok, rows_mm, x1_ok, ms_ok, y_fin, fw_ok = map(
            sem, ["sig_ok", "relu_ok", "mg_ok", "rows_mm", "x1_ok", "ms_ok", "y_fin", "fw_ok"])

        apart_sem = sem("apart")

        def apart(engine):
            engine.sem_inc(apart_sem, 1)

        block = ctx.enter_context(nc.Block())

        @block.sync
        def _(sp):
            def load(b, i, src):
                if b >= RS:
                    sp.wait_ge(w_ok, b + WS * i - RS + 1)
                    if not isinstance(i, int):
                        apart(sp)
                dst = raw[:, b % RS, :]
                if len(src.shape) == 3:
                    dst = dst.rearrange("p (k n) -> p k n", k=KT)
                sp.dma_start(dst, src).then_inc(raw_in[b % RS], 16)

            def cols(view, c):
                return view[:, :, bass.ds(c, 128)]

            cflat = arena[:, O_CONST:O_CONST + 128 * len(CONSTS)]
            sp.dma_start(cflat[:, 0:128], shape_consts[:, 0, :]).then_inc(ident_in, 16)
            for t in range(2):
                sp.dma_start(xn[:, t, :], x_v[:, t, :]).then_inc(x_in[t], 16)
            sp.dma_start(prow[PR_CONV:PR_MIX, :], conv_w[0].rearrange("t (b p) -> (t b) p", p=P)).then_inc(params_in, 16)
            sp.dma_start(prow[PR_MIX:PR_GATE, :], norm_mix_w[0].rearrange("(b p) -> b p", p=P)).then_inc(params_in, 16)
            sp.dma_start(prow[PR_GATE:PR_MLP, :], b_gate[0].rearrange("(b p) -> b p", p=P)).then_inc(params_in, 16)
            sp.dma_start(prow[PR_MLP:P, :], norm_mlp_w[0].rearrange("(b p) -> b p", p=P)).then_inc(params_in, 16)
            for t in range(2, TT):
                sp.dma_start(xn[:, t, :], x_v[:, t, :]).then_inc(x_in[t], 16)
            sp.dma_start(wbeta.rearrange("p (k n) -> p k n", k=KT),
                         w_in_v[:, :, COL_BETA:COL_BETA + 2 * NH]).then_inc(wb_in, 16)
            load(0, 0, cols(w_in_v, COL_CONV))
            load(1, 0, cols(w_in_v, COL_CONV + 128))
            sp.dma_start(cflat[:, 128:], shape_consts[:, 1:, :].rearrange("p a b -> p (a b)")).then_inc(consts_in, 16)
            sp.dma_start(alog, a_log[0:1, :].to_broadcast([P, NH])).then_inc(small_in, 16)
            sp.dma_start(dtb, dt_bias[0:1, :].to_broadcast([P, NH])).then_inc(small_in, 16)
            sp.dma_start(dnw, dn_norm_w.rearrange("a p -> p a")).then_inc(small_in, 16)
            sp.dma_start(sinks_all, attn_sinks[0:1, :].to_broadcast([P, 16])).then_inc(small_in, 16)
            for b in range(2, WS):
                load(b, 0, cols(w_in_v, COL_CONV + 128 * b))
            with sp.Fori(0, N_CONV // WS - 1) as i:
                for k in range(WS):
                    load(WS + k, i, cols(w_in_v, i * 512 + (COL_CONV + 512 + 128 * k)))
            with sp.Fori(0, TT) as t:
                for k, c in enumerate((COL_DZ, COL_DZ + 128, COL_Q, COL_Q + 128)):
                    load(B_DN + k, t, cols(w_in_v, t * 256 + c))
            load(B_KV, 0, cols(w_in_v, COL_K))
            load(B_KV + 1, 0, cols(w_in_v, COL_V))
            with sp.Fori(0, N_GATE // WS) as i:
                for k in range(WS):
                    load(B_GATE + k, i, cols(w_in_v, i * 512 + (COL_GATE + 128 * k)))
            for b0, view in ((B_BRD, brd_v), (B_BRA, bra_v)):
                with sp.Fori(0, N_BR // WS) as i:
                    for k in range(WS):
                        load(b0 + k, i, cols(view, i * 512 + 128 * k))
            sp.wait_ge(ya_ok, S // C)
            sp.dma_start(x1[:, :, :], x_v[:, :, :]).then_inc(x_again, 16)
            with sp.Fori(0, N_OUT // WS) as i:
                for k in range(WS):
                    load(B_OUT + k, i, w_out[0, bass.ds(i * 512 + 128 * k, 128), :])
            sp.dma_start(fw, final_norm_w.unsqueeze(0).to_broadcast([P, D])).then_inc(fw_ok, 16)
            with sp.Fori(0, N_UP // WS) as i:
                for k in range(WS):
                    load(B_UP + k, i, cols(up_v, i * 512 + 128 * k))
            with sp.Fori(0, N_DOWN // WS) as i:
                for k in range(WS):
                    load(B_DOWN + k, i, w_mlp_down[0, bass.ds(i * 512 + 128 * k, 128), :])
            for t in range(TT - 1):
                sp.wait_ge(y_fin, t + 1)
                sp.dma_start(out_v[:, t, :], x1[:, t, :]).then_inc(out_sent, 16)
            for n in range(2):
                cut = slice(512 * n, 512 * n + 512)
                sp.wait_ge(y_fin, TT + n)
                sp.dma_start(out_v[:, TT - 1, cut], x1[:, TT - 1, cut]).then_inc(out_sent, 16)
            sp.wait_ge(out_sent, 16 * (TT + 1))

        @block.gpsimd
        def _(pool):
            def lo(b, i=0):
                pool.wait_ge(w_hi_ok, b + WS * i + 1)
                pool.tensor_tensor(w_lo[:, b % WS, :], raw[:, b % RS, :], w_hi[:, b % WS, :].bitcast(F32),
                                   ALU.subtract).then_inc(w_ok, 1)

            pool.wait_ge(w_ok, 1)
            for k in range(1, WS):
                lo(k)
            with pool.Fori(1, N_CONV // WS + 1) as i:
                for k in range(WS):
                    lo(k, i)
            with pool.Fori(0, TT) as t:
                pool.wait_ge(kq_ok, t * 2 + 2)
                pool.wait_ge(eg_ok, t + 1)
                for c in range(2):
                    for s, part in ((0, c), (1, 1 - c)):
                        pool.tensor_tensor(KD[:, :, c, part, :], KQ[:, :, s, C * c:C * c + C],
                                           EG[:, :, C * c:C * c + C], ALU.mult).then_inc(kdq_ok, 1)
                for k in range(WS):
                    lo(B_DN + WS + k, t)
            lo(B_KV + WS)
            lo(B_KV + WS + 1)
            with pool.Fori(0, S // P) as s:
                for c in range(2):
                    pool.wait_ge(rden_ok, s * 2 + (c + 1))
                    pool.tensor_tensor(PR, PR, col(den), ALU.mult).then_inc(pn_ok, 1)
                    if c:
                        pool.wait_ge(dz_ok, 2)
                        y = yd[:, :, bass.ds(s * 128, 128)].rearrange("p (b k) n -> p k b n", k=2)
                        z = arena[:, QKV:QKV + 8 * S].rearrange("p (k s b n) -> p s k b n", k=2, s=4, b=4)
                        pool.tensor_tensor(y, y, z[:, bass.ds(s, 1), :, :, :].rearrange("p s k b n -> p (s k) b n"),
                                           ALU.mult).then_inc(ydz_ok, 1)
                    lo(B_GATE + WS + 2 * c, s)
                    lo(B_GATE + WS + 2 * c + 1, s)
            with pool.Fori(0, (B_END - B_BRD) // WS - 1) as i:
                for k in range(WS):
                    lo(B_BRD + WS + k, i)

        @block.tensor
        def _(pe):
            def products(out_ap, lhs, rhs, first, last):
                m = None
                for n, (a, b) in enumerate(((0, 0), (0, 1), (1, 0))):
                    m = pe.matmul(out_ap, lhs[a], rhs[b], start=first and n == 0, stop=last and n == 2)
                return m

            def part_f(b, i, k0, k1, tiles=None, free=False):
                f = b if b < B_OUT else b - N_OUT
                if k0 == 0:
                    pe.wait_ge(w_ok, b + WS * i + 1)
                    if f >= 2:
                        pe.wait_ge(blk_read, f + WS * i - 1)
                for k in range(k0, k1):
                    w = [h[:, b % WS, 128 * k:128 * k + 128] for h in (w_hi, w_lo)]
                    if tiles is not None:
                        pe.wait_ge(a_ok, tiles + k + 1)
                    m = products(ps[:, f % 2, :], w, (act_hi[:, k, :], act_lo[:, k, :]), k == 0, k == KT - 1)
                    if free and k < KT - 1:
                        m.then_inc(a_free, 1)
                if k1 == KT:
                    m.then_inc(blk_mm, 1)

            def block_f(b, i=0, tiles=None, free=False):
                part_f(b, i, 0, KT, tiles, free)

            def rows_t(b, slot, t, first, last, halves=(0, 1)):
                a = [h[:, slot, 128 * t:128 * t + 128] for h in (act_hi, act_lo)]
                for n in halves:
                    w = [h[:, b % WS, 512 * n:512 * n + 512] for h in (w_hi, w_lo)]
                    m = products(ps[:, 2 * t + n, :], a, w, first, last)
                return m

            def block_t(b, i, slot, tile, read=None):
                pe.wait_ge(w_ok, b + WS * i + 1)
                pe.wait_ge(a_ok, tile)
                for t in range(TT) if read is None else (1, 2, 3, 0):
                    if t == 0 and read is not None:
                        pe.wait_ge(blk_read, read)
                    m = rows_t(b, slot, t, read is not None, False)
                m.then_inc(blk_mm, 1)

            def last_blocks_t(b_end, slot0, tiles):
                pe.wait_ge(w_ok, b_end)
                pe.wait_ge(a_ok, tiles)
                for t, halves in ((0, (0, 1)), (1, (0, 1)), (2, (0, 1)), (3, (0,)), (3, (1,))):
                    for k in range(LAST):
                        m = rows_t(b_end - LAST + k, slot0 + k, t, False, k == LAST - 1, halves)
                    m.then_inc(*((blk_mm, LAST) if halves == (1,) else (rows_mm, 1)))

            def transposes_in(tiles):
                for t in range(TT):
                    pe.wait_ge(xn_ok, tiles + t + 1)
                    for k in range(KT):
                        m = pe.transpose(ps[:, k, 128 * t:128 * t + 128], xn[:, t, 128 * k:128 * k + 128], const["ident"])
                        if t == TT - 1:
                            m.then_inc(xt_mm, 1)

            pe.wait_ge(ident_in, 16)
            pe.wait_ge(params_in, 4 * 16)
            pe.transpose(ps[:, 0, 0:128], prow, const["ident"]).then_inc(par_mm, 1)
            pe.wait_ge(par_ok, 1)
            transposes_in(0)
            block_f(0, 0, 0)
            pe.wait_ge(wb_ok, 1)
            for k in range(KT):
                w = [wb[:, 2 * NH * k:2 * NH * (k + 1)] for wb in (wb_hi, wb_lo)]
                m = products(ps[0:2 * NH, 2, :], w, (act_hi[:, k, :], act_lo[:, k, :]), k == 0, k == KT - 1)
            m.then_inc(bd_mm, 1)
            part_f(1, 0, 0, 4)
            pe.wait_ge(bd_ok, 1)
            for t in range(TT):
                m = pe.transpose(ps[:, 3, 16 * t:16 * t + 16], bd_rows[:, 128 * t:128 * t + 128], const["ident"][0:16, 0:16])
            m.then_inc(bdt_mm, 1)
            part_f(1, 0, 4, KT)
            for b in range(2, WS):
                block_f(b)
            with pe.Fori(0, N_CONV // WS - 2) as i:
                for k in range(WS):
                    block_f(WS + k, i)
            pe.wait_ge(consts_in, 16)
            pe.wait_ge(g_ok, 1)
            for n, name in enumerate(("tri", "later")):
                m = pe.matmul(ps[:, 3, 32 * n:32 * n + 32], const[name], dec, start=n == 0, stop=True,
                              skip_group_check=True)
            m.then_inc(gc_mm, 1)
            for b in range(N_CONV - WS, N_CONV - 1):
                block_f(b)

            def quarters(t, js):
                for j in js:
                    part_f(B_DN + j // 4, t, 2 * (j % 4), 2 * (j % 4) + 2)

            def square_sums(t, n):
                pe.wait_ge(sq_ok, t * 2 + (n + 1))
                if n == 1 and not (isinstance(t, int) and t == 0):
                    pe.wait_ge(s_upd, t * 4)
                for g in range(HALVES):
                    m = pe.matmul(ps[:, 4 + 2 * n + g, :], const["ones"], (X, L)[n][:, GH * g:GH * g + GH, :],
                                  start=True, stop=True)
                m.then_inc(ss_mm, 1)

            def decay_rows(t):
                pe.wait_ge(g_now_ok, t + 1)
                pe.wait_ge(lns_ok, t * 2 + 2)
                for h in range(NH):
                    m = pe.matmul(heads(6)[:, h, :], g_now[:, h:h + 1].to_broadcast([P, 128]), const["tri"],
                                  start=h % GH == 0, stop=True, skip_group_check=True)
                m.then_inc(grow_mm, 1)

            def turn(t, q_start, q_gram, q_kt, q_levels, q_scan, first=False, last=False):
                quarters(t, q_start)
                pe.wait_ge(kq_ok, t * 2 + 2)
                pe.wait_ge(lns_ok, t * 2 + 1)
                if first:
                    pe.wait_ge(gc_ok, 2)
                    pe.wait_ge(s0_ok, 1)
                else:
                    pe.wait_ge(yd_ok, t * 2)
                for h in range(NH):
                    m = pe.matmul(ps[:, 2 + h // 2, 256 * (h % 2):256 * (h % 2) + 256], KQ[:, h, 0, :],
                                  KQ[:, h, :, :], start=h % 2 == 0, stop=True, skip_group_check=True)
                m.then_inc(gram_mm, 1)
                quarters(t, q_gram)
                pe.wait_ge(vs_ok, t + 1)
                pe.wait_ge(l_raw, t + 1)
                pe.wait_ge(int_ok, t + 1)
                for h in range(NH):
                    m = pe.transpose(heads(2)[:, h, :], VS[:, h, :], const["ident"])
                m.then_inc(vt_mm, 1)
                for h in range(NH):
                    m = pe.transpose(heads(4)[:, h, :], KQ[:, h, 0, :], const["ident"])
                m.then_inc(kt_mm, 1)
                quarters(t, q_kt)
                for lv in range(len(LEVELS)):
                    last_level = lv == len(LEVELS) - 1
                    for g in range(HALVES):
                        if lv == 0:
                            pe.wait_ge(l_ok, t + 1)
                            pe.wait_ge(t0_ok, t * 2 + (g + 1))
                            pe.wait_ge(vtok_ok, t + 1)
                        else:
                            pe.wait_ge(t_upd, t * 10 + (2 * lv - 1 + g))
                        for h in range(GH * g, GH * g + GH):
                            m = pe.matmul(heads(2)[:, h, :], L[:, h, :], T[:, h, :], start=h % GH == 0, stop=True,
                                          skip_group_check=True)
                        m.then_inc(y_mm, 1)
                    for g in range(HALVES):
                        pe.wait_ge(y_ok, t * 10 + (2 * lv + g + 1))
                        if lv == 0:
                            pe.wait_ge(eg_ok, t + 1)
                        if last_level:
                            pe.wait_ge(kdec_ok, t * 2 + (g + 1))
                        for h in range(GH * g, GH * g + GH):
                            if last_level:
                                m = pe.matmul(heads(4)[:, h, :], X[:, h, :], Y[:, h, :], start=h % GH == 0,
                                              stop=True, skip_group_check=True)
                            else:
                                m = pe.matmul(heads(6)[:, h, :], Y[:, h, :], X[:, h, :], start=h % GH == 0,
                                              stop=True, skip_group_check=True)
                        m.then_inc(xt2_mm, 1)
                    quarters(t, q_levels[lv])
                pe.wait_ge(kdq_ok, t * 4 + 4)
                for c in range(2):
                    p0 = C * c
                    own, other = slice(p0, p0 + C), slice(C - p0, 2 * C - p0)
                    for g in range(HALVES):
                        if c:
                            pe.wait_ge(s_upd, t * 4 + (1 + g))
                            pe.wait_ge(o_ok, t * 4 + (1 + g))
                        for h in range(GH * g, GH * g + GH):
                            m = pe.matmul(heads(2)[:, h, :], KD[:, h, c, :, :].rearrange("p s n -> p (s n)"), ST[:, h, :],
                                          start=h % GH == 0, stop=False, skip_group_check=True)
                        m.then_inc(kq_mm, 1)
                    if c == 0:
                        quarters(t, q_scan)
                        pe.wait_ge(tb_ok, t + 1)
                    for g in range(HALVES):
                        pe.wait_ge(r_ok, t * 4 + (2 * c + g + 1))
                        if c:
                            pe.wait_ge(vn_ok, t * 4 + (1 + g))
                        for h in range(GH * g, GH * g + GH):
                            m = pe.matmul(heads(4)[:, h, :], T[own, h, :], R[own, h, :],
                                          start=h % GH == 0, stop=True, skip_group_check=True)
                        m.then_inc(vn_mm, 1)
                    for g in range(HALVES):
                        pe.wait_ge(vn_ok, t * 4 + (2 * c + g + 1))
                        for h in range(GH * g, GH * g + GH):
                            m = pe.matmul(heads(6)[:, h, :], TAILK[own, h, :], VN[own, h, :],
                                          start=h % GH == 0, stop=True, skip_group_check=True)
                        m.then_inc(su_mm, 1)
                        for h in range(GH * g, GH * g + GH):
                            m = pe.matmul(heads(2)[other, h, :], INT[own, h, p0:p0 + C], VN[own, h, :],
                                          start=False, stop=True, skip_group_check=True)
                        m.then_inc(o_mm, 1)
                if last:
                    quarters(t, (13, 14, 15))
                    block_f(B_KV)
                else:
                    square_sums(t + 1, 0)
                    quarters(t, (13,))
                    square_sums(t + 1, 1)
                    quarters(t, (14, 15))
                    decay_rows(t + 1)
                pe.wait_ge(on_ok, t + 1)
                for h in range(NH):
                    m = pe.transpose(heads(2)[:, h, :], O[:, h, :], const["ident"])
                m.then_inc(on_mm, 1)

            square_sums(0, 0)
            square_sums(0, 1)
            block_f(N_CONV - 1)
            quarters(0, (0, 1, 2, 3, 4, 5))
            decay_rows(0)
            turn(0, (6,), (7, 8), (9,), ((10,), (11,), (12,), (), ()), (), first=True)
            usual = (0, 1), (2, 3, 4), (5, 6), ((7,), (8,), (9,), (10,), (11,)), (12,)
            with pe.Fori(1, TT - 1) as t:
                turn(t, *usual)
            turn(TT - 1, *usual, last=True)
            block_f(B_KV + 1)
            pe.wait_ge(yd_ok, 2 * TT)
            pe.wait_ge(s_upd, 4 * TT)

            def attend(n, c, s, before, last):
                pe.wait_ge(qs_ok, n + 1)
                pe.wait_ge(ks_ok, n + 1)
                for e in range(2):
                    for r in range(4):
                        m = pe.matmul(ps[:, 2 + e, 128 * r:128 * r + 128],
                                      qs[c][64 * e:64 * e + 64, 2 * r:2 * r + 2, :].rearrange("p a b -> p (a b)"),
                                      kvs[c][64 * e:64 * e + 64, r // 2, :], start=r == 0, stop=True,
                                      skip_group_check=True)
                m.then_inc(sc_mm, 1)
                block_f(B_GATE + 2 * c, s)
                pe.wait_ge(vals_ok, n + 1)
                pe.transpose(ps[:, 7, 0:128], kvs[c][:, 2, :], const["ident"]).then_inc(vw_mm, 1)
                second = (B_GATE + 2 * c + 1, s)
                part_f(*second, 0, 4, None, last)
                pe.wait_ge(pn_ok, n + 1)
                for a in range(8):
                    m = pe.transpose(heads(4)[:, a, :], PR[:, a, :], const["ident"])
                m.then_inc(pt_mm, 1)
                part_f(*second, 4, 6, None, last)
                if before:
                    pe.wait_ge(ya_ok, n)
                pe.wait_ge(vw_ok, n + 1)
                pe.wait_ge(pt_ok, n + 1)
                for e in range(2):
                    for j in range(2):
                        m = pe.matmul(ps[64 * e:64 * e + 64, 6, 256 * j:256 * j + 256], vt2[c][:, 64 * j:64 * j + 64],
                                      PT[:, 4 * e + 2 * j:4 * e + 2 * j + 2, :], start=j == 0, stop=True,
                                      skip_group_check=True)
                m.then_inc(pv_mm, 1)
                part_f(*second, 6, 8, None, last)

            attend(0, 0, 0, False, False)
            attend(1, 1, 0, True, False)
            with pe.Fori(1, S // P - 1) as s:
                for c in range(2):
                    attend(s * 2 + c, c, s, True, False)
            attend(6, 0, 3, True, False)
            attend(7, 1, 3, True, True)

            for b0, tiles in ((B_BRD, T_DELTA), (B_BRA, T_ATT)):
                for k in range(N_BR):
                    block_f(b0 + k, 0, tiles if k == 0 else None, k == N_BR - 1)
            for k in range(N_OUT - LAST):
                block_t(B_OUT + k, 0, k, T_MERGED + k + 1, B_OUT if k == 0 else None)
            last_blocks_t(B_UP, N_OUT - LAST, T_MERGED + N_OUT)
            pe.wait_ge(x1_ok, TT + 1)
            transposes_in(TT)
            block_f(B_UP, 0, T_MLP)
            for k in range(1, WS):
                block_f(B_UP + k)
            with pe.Fori(0, N_UP // WS - 2) as i:
                for k in range(WS):
                    block_f(B_UP + WS + k, i)
            for k in range(WS):
                block_f(B_UP + N_UP - WS + k, 0, None, k == WS - 1)
            for k in range(WS):
                block_t(B_DOWN + k, 0, k, T_SQ + k + 1, B_DOWN - N_OUT if k == 0 else None)
            with pe.Fori(1, N_DOWN // WS - 1) as i:
                for k in range(WS):
                    block_t(B_DOWN + k, i, k, i * WS + (T_SQ + k + 1))
            block_t(B_END - WS, 0, 0, T_SQ + N_DOWN - LAST)
            last_blocks_t(B_END, WS - LAST, T_SQ + N_DOWN)

        @block.scalar
        def _(act):
            def hi(b, i=0):
                act.wait_ge(raw_in[b % RS], i * (16 * WS // RS) + 16 * (b // RS + 1))
                if b >= WS:
                    act.wait_ge(blk_mm, i * WS + (b - WS + 1))
                act.activation(w_hi[:, b % WS, :], raw[:, b % RS, :], ACT.Copy).then_inc(w_hi_ok, 1)

            def row_scale(done, t, rows, junk, sums):
                act.activation(junk, rows, ACT.Square, accum_out=ss[:, t:t + 1]).then_inc(ss_ok, 1)
                row_scale_end(done, t, sums, eps_c)

            def row_scale_end(done, t, sums, bias):
                act.wait_ge(ss_ok, sums + t + 1)
                act.activation(rstd[:, t:t + 1], ss[:, t:t + 1], ACT.Ln, bias=bias, scale=1.0 / D).then_inc(ln_ok, 1)
                act.wait_ge(ln_ok, done + t + 1)
                act.activation(rstd[:, t:t + 1], rstd[:, t:t + 1], ACT.Exp, scale=-0.5).then_inc(rstd_ok, 1)

            def norm_hi(done, row):
                for k in range(KT):
                    act.wait_ge(xt_mm, done + k + 1)
                    act.activation(act_hi[:, k, :], ps[:, k, :], ACT.Identity,
                                   scale=par[:, row + k:row + k + 1]).then_inc(a_hi_ok, 1)

            act.preload_act_table_set("natural_log_exp_and_others")
            act.wait_ge(eps_ok, 1)
            for t in range(TT):
                act.wait_ge(x_in[t], 16)
                row_scale(0, t, xn[:, t, :], flat(O_JUNK0 + D * t, D), 0)
            hi(0)
            act.wait_ge(par_ok, 1)
            norm_hi(0, PR_MIX)
            hi(1)
            act.wait_ge(wb_in, 16)
            act.activation(wb_hi[:, :], wbeta, ACT.Copy).then_inc(wb_hi_ok, 1)
            hi(2)
            hi(3)
            act.wait_ge(sm, 3)
            act.activation(tmp[1], tmp[1], ACT.Exp).then_inc(sm_act, 1)
            act.activation(beta3, bd_cols[:, :, 0:NH], ACT.Exp, scale=-1.0).then_inc(sm_act, 1)
            act.wait_ge(small_in, 4 * 16)
            act.activation(alog, alog, ACT.Exp).then_inc(sm_act, 1)
            act.wait_ge(sm_act, 1)
            act.activation(tmp[1], tmp[1], ACT.Ln, bias=1.0).then_inc(sm_act, 1)
            def conv_silu(k, i):
                act.wait_ge(blk_read, i * WS + (k + 1))
                if not isinstance(i, int):
                    apart(act)
                q = qkv[:, bass.ds(i * WS + k, 1), :]
                act.activation(q, q, ACT.Silu).then_inc(conv_ok, 1)
                hi(WS + k, i)

            def squares(t):
                for n in range(2):
                    act.activation((X, L)[n], qkv[:, 8 - 8 * n:16 - 8 * n, bass.ds(t * 128, 128)],
                                   ACT.Square).then_inc(sq_ok, 1)

            def norm_ln(t, n):
                act.wait_ge(ss_mm, t * 2 + (n + 1))
                act.activation((X, L)[n], heads(4 + 2 * n), ACT.Ln, bias=eps_c).then_inc(lns_ok, 1)

            def norm_exp(t, n):
                act.wait_ge(lns_ok, t * 2 + (n + 1))
                act.activation((X, L)[n], (X, L)[n], ACT.Exp, scale=-0.5,
                               bias=(zero_c, lnq_c)[n]).then_inc(rn_ok, 1)

            with act.Fori(0, N_CONV // WS - 1) as i:
                for k in range(WS):
                    conv_silu(k, i)
            for k in range(WS):
                conv_silu(k, N_CONV // WS - 1)
                if k == 0:
                    act.wait_ge(conv_ok, 16)
                    squares(0)
            act.preload_act_table_set("natural_log_exp_and_others")
            for step in (norm_ln, norm_exp):
                for n in range(2):
                    step(0, n)
            act.wait_ge(gc_ok, 1)
            act.activation(tail, ps[:, 3, 32:64], ACT.Exp).then_inc(gc_ok, 1)
            act.wait_ge(conv_ok, N_CONV)

            def filler(t, k):
                act.wait_ge(blk_mm, t * WS + (B_DN + k + 1))
                if not isinstance(t, int):
                    apart(act)
                act.activation(qkv[:, 4 * k:4 * k + 4, bass.ds(t * 128, 128)],
                               ps[:, k % 2, :].rearrange("p (a n) -> p a n", a=4), ACT.Copy).then_inc(blk_read, 1)
                hi(B_DN + WS + k, t)

            def turn(t, last=False):
                now = bass.ds(t * 128, 128)
                act.wait_ge(arg_ok, t + 1)
                act.activation(EG, heads(6), ACT.Exp).then_inc(eg_ok, 1)
                act.activation(VS, qkv[:, 16:24, now], ACT.Copy).then_inc(vs_ok, 1)
                for n in range(2):
                    act.wait_ge(darg_ok, t * 2 + (n + 1))
                    act.activation((L, INT)[n], (L, INT)[n], ACT.Exp).then_inc(dexp_ok, 1)
                act.wait_ge(kq_ok, t * 2 + 2)
                filler(t, 0)
                act.wait_ge(vt_mm, t + 1)
                act.activation(VTOK, heads(2), ACT.Copy).then_inc(vtok_ok, 1)
                filler(t, 1)
                if not last:
                    act.wait_ge(xt2_mm, t * 10 + 10)
                    act.wait_ge(t_upd, t * 10 + 8)
                    squares(t + 1)
                filler(t, 2)
                for c in range(2):
                    other = slice(C - C * c, 2 * C - C * c)
                    own = slice(C * c, C * c + C)
                    for g in range(HALVES):
                        hs = slice(GH * g, GH * g + GH)
                        act.wait_ge(vn_mm, t * 4 + (2 * c + g + 1))
                        act.activation(VN[own, hs, :], heads(4)[own, hs, :], ACT.Copy).then_inc(vn_ok, 1)
                    for g in range(HALVES):
                        hs = slice(GH * g, GH * g + GH)
                        act.wait_ge(o_mm, t * 4 + (2 * c + g + 1))
                        act.activation(O[other, hs, :], heads(2)[other, hs, :], ACT.Copy).then_inc(o_ok, 1)
                if not last:
                    norm_ln(t + 1, 0)
                    norm_exp(t + 1, 0)
                act.wait_ge(oss_ok, t + 1)
                act.activation(ors, oss, ACT.Ln, scale=1.0 / 128, bias=eps_c).then_inc(oln_ok, 1)
                act.wait_ge(oln_ok, t + 1)
                act.activation(ors, ors, ACT.Exp, scale=-0.5).then_inc(ors_ok, 1)
                if not last:
                    norm_ln(t + 1, 1)
                    norm_exp(t + 1, 1)
                filler(t, 3)
                act.wait_ge(on_mm, t + 1)
                if not last:
                    apart(act)
                for c in range(2):
                    act.activation(yd[:, :, bass.ds(t * 128 + C * c, C)], heads(2)[:, :, C - C * c:2 * C - C * c],
                                   ACT.Identity, scale=dnw).then_inc(yd_ok, 1)

            with act.Fori(0, TT - 1) as t:
                turn(t)
            turn(TT - 1, True)

            act.wait_ge(kv_pad, 1)
            act.wait_ge(blk_mm, B_KV + 1)
            for j in range(2):
                for e in range(2):
                    m = act.activation(kvt[64 * e:64 * e + 64, j, C:], ps[64 * j:64 * j + 64, 0, :], ACT.Copy)
            m.then_inc(blk_read, 1)
            act.wait_ge(blk_read, B_KV + 1)

            queries = arena[:, QKV:QKV + 24 * S].rearrange("p (b s t u q) -> p b s t u q", b=6, s=4, t=4, u=2)

            def stage_values(n, c):
                act.activation(kvs[c][:, 2, :], kvt[:, 2, bass.ds(n * C, 128)], ACT.Copy).then_inc(vals_ok, 1)

            def stage(n, c, s):
                act.activation(qs[c].rearrange("p (t j) q -> p j t q", j=2),
                               queries[:, 2:4, bass.ds(s, 1), :, c, :].rearrange("p b s t q -> p b (s t) q"),
                               ACT.Copy).then_inc(qs_ok, 1)
                act.activation(kvs[c][:, 0:2, :], kvt[:, 0:2, bass.ds(n * C, 128)], ACT.Copy).then_inc(ks_ok, 1)

            def attend(n, c, s, first=False, last=False):
                act.wait_ge(pe_ok, n + 1)
                act.activation(PR, PR, ACT.Exp).then_inc(exp_ok, 1)
                act.wait_ge(esd_ok, n + 1)
                act.activation(es, es, ACT.Exp).then_inc(es_ok, 1)
                if not last:
                    stage(n + 1, 1 - c, s + c)
                    stage_values(n + 1, 1 - c)
                act.wait_ge(vw_mm, n + 1)
                act.activation(vt2[c], ps[:, 7, 0:128], ACT.Copy).then_inc(vw_ok, 1)
                if first:
                    for j in range(2):
                        act.activation(qkv[:, 4 * j:4 * j + 4, :], qkv[:, 4 * j:4 * j + 4, :], ACT.Silu).then_inc(dz_ok, 1)
                    act.preload_act_table_set("exp_and_others")
                hi(B_GATE + WS + 2 * c, s)
                if last:
                    act.wait_ge(ydz_ok, 4)
                    for k in range(KT):
                        act.wait_ge(a_free, k + 1) if k < KT - 1 else act.wait_ge(blk_mm, B_BRD)
                        act.activation(act_hi[:, k, :], yd[:, k, :], ACT.Copy).then_inc(a_hi_ok, 1)
                act.wait_ge(pv_mm, n + 1)
                apart(act)
                act.activation(yatt[:, :, bass.ds(n * C, C)], ps[:, 6, :].rearrange("p (h q) -> p h q", h=KT),
                               ACT.Copy).then_inc(ya_ok, 1)
                hi(B_GATE + WS + 2 * c + 1, s)

            stage(0, 0, 0)
            act.wait_ge(blk_mm, B_KV + 2)
            act.activation(kvt[:, 2, C:], ps[:, 1, :], ACT.Copy).then_inc(blk_read, 1)
            act.wait_ge(blk_read, B_KV + 2)
            stage_values(0, 0)
            hi(B_KV + WS)
            hi(B_KV + WS + 1)
            attend(0, 0, 0, first=True)
            attend(1, 1, 0)
            with act.Fori(1, S // P - 1) as s:
                for c in range(2):
                    attend(s * 2 + c, c, s)
            attend(6, 0, 3)
            attend(7, 1, 3, last=True)

            act.wait_ge(blk_read, B_BRD)
            act.activation(gates[:, 8:16, :], gates[:, 8:16, :], ACT.Sigmoid).then_inc(sig_ok, 1)
            hi(B_BRD + WS)
            act.activation(gates[:, 0:8, :], gates[:, 0:8, :], ACT.Sigmoid).then_inc(sig_ok, 1)
            for k in range(1, N_BR - 1):
                hi(B_BRD + WS + k)
            act.wait_ge(ya_ok, S // C)
            for k in range(KT):
                act.wait_ge(a_free, KT - 1 + k + 1) if k < KT - 1 else act.wait_ge(blk_mm, B_BRA)
                act.activation(act_hi[:, k, :], yatt[:, k, :], ACT.Copy).then_inc(a_hi_ok, 1)
            for k in range(N_BR - 1, 2 * N_BR - 1):
                hi(B_BRD + WS + k)
            for k in range(KT):
                act.wait_ge(a_free, 2 * (KT - 1) + k + 1) if k < KT - 1 else act.wait_ge(blk_mm, B_OUT)
                act.wait_ge(mg_ok, k + 1)
                act.activation(act_hi[:, k, :], gates[:, k, :], ACT.Copy).then_inc(a_hi_ok, 1)
            for k in range(2 * N_BR - 1, 2 * N_BR + N_OUT - WS + 1):
                hi(B_BRD + WS + k)
            act.preload_act_table_set("natural_log_exp_and_others")

            def rows_scale(p):
                for t in range(TT - 1):
                    act.wait_ge(x1_ok, p * (TT + 1) + t + 1)
                    row_scale(TT + p * TT, t, x1[:, t, :], flat(O_JUNK1 + D * t, D), TT + p * (TT + 1))
                t = TT - 1
                for n, acc in enumerate((ms_half, ss[:, t:t + 1])):
                    act.wait_ge(x1_ok, p * (TT + 1) + t + n + 1)
                    act.activation(flat(O_JUNK1 + D * t + 512 * n, 512), x1[:, t, 512 * n:512 * n + 512], ACT.Square,
                                   accum_out=acc).then_inc(ss_ok, 1)
                act.wait_ge(ms_ok, p + 1)
                row_scale_end(TT + p * TT, t, TT + p * (TT + 1) + 1, ms_half)

            rows_scale(0)
            hi(B_UP + 1)
            hi(B_UP + 2)
            norm_hi(KT, PR_MLP)
            hi(B_UP + WS - 1)

            def relu(k, i):
                act.wait_ge(blk_mm, i * WS + (B_UP + k + 1))
                if not isinstance(i, int):
                    apart(act)
                act.activation(a_t[:, bass.ds(i * WS + k, 1), :].rearrange("p a n -> p (a n)"), ps[:, k % 2, :],
                               ACT.Relu).then_inc(relu_ok, 1)

            with act.Fori(0, N_UP // WS - 1) as i:
                for k in range(WS):
                    relu(k, i)
                    hi(B_UP + WS + k, i)

            def squares_hi(k, i=0):
                act.wait_ge(blk_read, i * WS + (B_UP - N_OUT + k + 1))
                if k < WS:
                    act.wait_ge(a_free, 3 * (KT - 1) + k + 1)
                else:
                    act.wait_ge(blk_mm, i * WS + (B_DOWN + k - WS + 1))
                if not isinstance(i, int):
                    apart(act)
                act.activation(act_hi[:, k % WS, :], a_t[:, bass.ds(i * WS + k, 1), :].rearrange("p a n -> p (a n)"),
                               ACT.Copy).then_inc(a_hi_ok, 1)

            for k in range(WS):
                if k == WS - 1:
                    for j in range(WS):
                        squares_hi(j)
                relu(k, N_UP // WS - 1)
                hi(B_DOWN + k)
            with act.Fori(0, N_DOWN // WS - 1) as i:
                for k in range(WS):
                    hi(B_DOWN + WS + k, i)
                    squares_hi(WS + k, i)
            rows_scale(1)

        @block.vector
        def _(dve):
            def norm_lo(done, row):
                for k in range(KT):
                    dve.wait_ge(a_hi_ok, done + k + 1)
                    dve.scalar_tensor_tensor(out=act_lo[:, k, :], in0=ps[:, k, :], scalar=par[:, row + k:row + k + 1],
                                             in1=act_hi[:, k, :].bitcast(F32), op0=ALU.mult,
                                             op1=ALU.subtract).then_inc(a_ok, 1)

            def split_lo(done, src, k0, k1):
                for k in range(k0, k1):
                    dve.wait_ge(a_hi_ok, done + k + 1)
                    dve.tensor_tensor(act_lo[:, k, :], src[:, k, :], act_hi[:, k, :].bitcast(F32),
                                      ALU.subtract).then_inc(a_ok, 1)

            dve.memset(eps_c, EPS)
            dve.memset(zero_c, 0.0)
            dve.memset(lnq_c, LN_Q_SCALE).then_inc(eps_ok, 1)
            dve.wait_ge(par_mm, 1)
            dve.tensor_copy(par, ps[:, 0, 0:128]).then_inc(par_ok, 1)
            for t in range(TT):
                dve.wait_ge(rstd_ok, t + 1)
                dve.tensor_scalar(xn[:, t, :], xn[:, t, :], rstd[:, t:t + 1], None, ALU.mult).then_inc(xn_ok, 1)
            dve.wait_ge(w_hi_ok, 1)
            dve.tensor_tensor(w_lo[:, 0, :], raw[:, 0, :], w_hi[:, 0, :].bitcast(F32), ALU.subtract).then_inc(w_ok, 1)
            dve.wait_ge(par_ok, 1)
            norm_lo(0, PR_MIX)
            dve.wait_ge(wb_hi_ok, 1)
            dve.tensor_tensor(wb_lo[:, :], wbeta, wb_hi[:, :].bitcast(F32), ALU.subtract).then_inc(wb_ok, 1)

            def conv(i, k):
                dve.wait_ge(blk_mm, i * WS + (k + 1))
                q = qkv[:, bass.ds(i * WS + k, 1), :].rearrange("p a n -> p (a n)")
                z = ps[:, k % 2, :]
                taps = [par[:, bass.ds(i * WS + (PR_CONV + 24 * j + k), 1)] for j in range(4)]
                dve.tensor_scalar(q, z, taps[3], None, ALU.mult).then_inc(conv_tap, 1)
                for j in (2, 1, 0):
                    d = 3 - j
                    dve.wait_ge(conv_tap, i * (3 * WS) + (3 * k + d))
                    m = dve.scalar_tensor_tensor(out=q[:, d:S], in0=z[:, 0:S - d], scalar=taps[j],
                                                 in1=q[:, d:S], op0=ALU.mult, op1=ALU.add)
                    m.then_inc(conv_tap if j else blk_read, 1)

            conv(0, 0)
            dve.wait_ge(bd_mm, 1)
            dve.tensor_copy(bd_rows, ps[0:2 * NH, 2, :]).then_inc(bd_ok, 1)
            dve.wait_ge(bdt_mm, 1)
            dve.wait_ge(small_in, 4 * 16)
            y3 = tmp[0].rearrange("p (t h) -> p t h", h=NH)

            def rows(a):
                return a.unsqueeze(1).to_broadcast([P, TT, NH])

            dve.tensor_tensor(y3, bd_cols[:, :, NH:2 * NH], rows(dtb), ALU.add).then_inc(sm, 1)
            dve.wait_ge(sm, 1)
            dve.tensor_scalar(tmp[1], tmp[0], -1.0, None, ALU.mult).then_inc(sm, 1)
            dve.wait_ge(sm, 2)
            dve.tensor_tensor(tmp[1], tmp[0], tmp[1], ALU.min).then_inc(sm, 1)
            dve.wait_ge(sm_act, 4)
            dve.wait_ge(sm, 3)
            dve.scalar_tensor_tensor(out=tmp[0], in0=tmp[0], scalar=0.0, in1=tmp[1], op0=ALU.max,
                                     op1=ALU.add).then_inc(sm, 1)
            dve.tensor_scalar(beta, beta, 1.0, None, ALU.add).then_inc(sm, 1)
            dve.wait_ge(sm, 5)
            dve.scalar_tensor_tensor(out=dec3, in0=y3, scalar=-1.0, in1=rows(alog), op0=ALU.mult,
                                     op1=ALU.mult).then_inc(g_ok, 1)
            dve.reciprocal(beta, beta).then_inc(sm, 1)
            for hl in range(2):
                rs = slice(64 * hl, 64 * hl + 64)
                dve.tensor_copy(sinks[rs, :].rearrange("p (e r) -> p e r", e=2),
                                sinks_all[rs, :].rearrange("p (r l e) -> p l e r", l=2, e=2)[:, hl]).then_inc(sink_ok, 1)
            for k in range(1, WS):
                conv(0, k)
            with dve.Fori(1, N_CONV // WS - 1) as i:
                for k in range(WS):
                    conv(i, k)
            dve.wait_ge(gc_mm, 1)
            dve.tensor_copy(gcol, ps[:, 3, 0:32]).then_inc(gc_ok, 1)
            dve.memset(arena[:, O_S:O_S + 1024], 0.0).then_inc(s0_ok, 1)
            for k in range(WS):
                conv(N_CONV // WS - 1, k)

            def decay_now(t):
                dve.tensor_copy(g_now, dec3[:, bass.ds(t, 1), :].rearrange("p a h -> p (a h)")).then_inc(g_now_ok, 1)

            def normalised(t, n):
                dve.wait_ge(rn_ok, t * 2 + (n + 1))
                dve.tensor_tensor(KQ[:, :, n, :], qkv[:, 8 - 8 * n:16 - 8 * n, bass.ds(t * 128, 128)], (X, L)[n],
                                  ALU.mult).then_inc(kq_ok, 1)

            dve.wait_ge(gc_ok, 1)
            dve.wait_ge(sm, 6)
            decay_now(0)
            normalised(0, 0)
            normalised(0, 1)

            def turn(t, last=False):
                def token_col(a3):
                    return col(a3[:, bass.ds(t, 1), :].rearrange("p a h -> p (a h)"))

                dve.wait_ge(grow_mm, t + 1)
                dve.tensor_tensor(INT, heads(6), token_col(gcol3), ALU.subtract).then_inc(arg_ok, 1)
                dve.wait_ge(arg_ok, t + 1)
                dve.tensor_tensor(L, mat("mask_l"), INT, ALU.subtract).then_inc(darg_ok, 1)
                dve.tensor_tensor(INT, mat("mask_t"), INT, ALU.add).then_inc(darg_ok, 1)
                dve.wait_ge(eg_ok, t + 1)
                dve.tensor_copy(gl3, EG[:, :, C - 1:2 * C:C]).then_inc(gl_ok, 1)
                grams = ps[:, 2:6, :].rearrange("p b (h s n) -> p (b h) s n", h=2, s=2)
                dve.wait_ge(gram_mm, t + 1)
                dve.wait_ge(dexp_ok, t * 2 + 1)
                dve.tensor_tensor(L, grams[:, :, 0, :], L, ALU.mult).then_inc(l_raw, 1)
                dve.wait_ge(dexp_ok, t * 2 + 2)
                dve.tensor_tensor(INT, grams[:, :, 1, :], INT, ALU.mult).then_inc(int_ok, 1)
                dve.wait_ge(l_raw, t + 1)
                dve.tensor_tensor(L, L, token_col(beta3), ALU.mult).then_inc(l_ok, 1)
                dve.wait_ge(l_ok, t + 1)
                dve.tensor_tensor(Y, L, mat("m1"), ALU.mult).then_inc(y1_ok, 1)
                dve.wait_ge(y1_ok, t + 1)
                dve.tensor_tensor(X, mat("ident"), Y, ALU.subtract).then_inc(x0_ok, 1)
                dve.wait_ge(x0_ok, t + 1)
                for g in range(HALVES):
                    hs = slice(GH * g, GH * g + GH)
                    dve.transpose(T[:, hs, :], X[:, hs, :]).then_inc(t0_ok, 1)
                for lv, name in enumerate(LEVELS):
                    for g in range(HALVES):
                        hs = slice(GH * g, GH * g + GH)
                        dve.wait_ge(y_mm, t * 10 + (2 * lv + g + 1))
                        dve.tensor_tensor(Y[:, hs, :], heads(2)[:, hs, :], mat(name, GH), ALU.mult).then_inc(y_ok, 1)
                    if lv in (1, 2):
                        hs = slice(GH * (lv - 1), GH * lv)
                        dve.wait_ge(kt_mm, t + 1)
                        dve.wait_ge(gc_ok, 2)
                        dve.tensor_tensor(TAILK[:, hs, :], heads(4)[:, hs, :],
                                          tail3[:, bass.ds(t, 1), hs].rearrange("p a h -> p (a h)").unsqueeze(2)
                                          .to_broadcast([P, GH, 128]), ALU.mult).then_inc(kdec_ok, 1)
                    for g in range(HALVES):
                        hs = slice(GH * g, GH * g + GH)
                        dve.wait_ge(xt2_mm, t * 10 + (2 * lv + g + 1))
                        if lv == len(LEVELS) - 1:
                            dve.tensor_tensor(T[:, hs, :], T[:, hs, :], heads(4)[:, hs, :], ALU.subtract).then_inc(t_upd, 1)
                        else:
                            dve.tensor_tensor(X[:, hs, :], X[:, hs, :], heads(6)[:, hs, :], ALU.subtract).then_inc(x_upd, 1)
                            dve.wait_ge(x_upd, t * 8 + (2 * lv + g + 1))
                            dve.transpose(T[:, hs, :], X[:, hs, :]).then_inc(t_upd, 1)
                dve.wait_ge(t_upd, t * 10 + 10)
                dve.tensor_tensor(T, T, token_col(beta3), ALU.mult).then_inc(tb_ok, 1)
                for c in range(2):
                    own = slice(C * c, C * c + C)
                    for g in range(HALVES):
                        hs = slice(GH * g, GH * g + GH)
                        dve.wait_ge(kq_mm, t * 4 + (2 * c + g + 1))
                        dve.wait_ge(vtok_ok, t + 1)
                        dve.tensor_tensor(R[own, hs, :], VTOK[own, hs, :], heads(2)[own, hs, :],
                                          ALU.subtract).then_inc(r_ok, 1)
                    for g in range(HALVES):
                        dve.wait_ge(su_mm, t * 4 + (2 * c + g + 1))
                        dve.wait_ge(gl_ok, t + 1)
                        for h in range(GH * g, GH * g + GH):
                            m = dve.scalar_tensor_tensor(out=ST[:, h, :], in0=ST[:, h, :], scalar=gl3[:, h, c:c + 1],
                                                         in1=heads(6)[:, h, :], op0=ALU.mult, op1=ALU.add)
                        m.then_inc(s_upd, 1)
                dve.wait_ge(o_ok, t * 4 + 4)
                dve.tensor_tensor(Y, O, O, ALU.mult).then_inc(osq_ok, 1)
                dve.wait_ge(osq_ok, t + 1)
                dve.tensor_reduce(oss, Y, AX_X, ALU.add).then_inc(oss_ok, 1)
                if not last:
                    decay_now(t + 1)
                    normalised(t + 1, 0)
                dve.wait_ge(ors_ok, t + 1)
                dve.tensor_tensor(O, O, col(ors), ALU.mult).then_inc(on_ok, 1)
                if not last:
                    normalised(t + 1, 1)

            with dve.Fori(0, TT - 1) as t:
                turn(t)
            turn(TT - 1, True)

            dve.memset(kvt[:, :, 0:C], 0.0).then_inc(kv_pad, 1)
            def attend(n, c, s, first=False, last=False):
                k0 = C if first else 0
                sc = heads(2)[:, :, k0:]
                prk = PR[:, :, k0:]
                w = 128 - k0
                dve.wait_ge(sc_mm, n + 1)
                dve.tensor_reduce(mx, sc, AX_X, ALU.max).then_inc(mx_ok, 1)
                dve.wait_ge(mx_ok, n + 1)
                dve.scalar_tensor_tensor(out=mx, in0=mx, scalar=HD ** -0.5, in1=sinks, op0=ALU.mult,
                                         op1=ALU.max).then_inc(m_ok, 1)
                dve.wait_ge(m_ok, n + 1)
                dve.scalar_tensor_tensor(out=prk, in0=sc, scalar=HD ** -0.5,
                                         in1=mx.unsqueeze(2).to_broadcast([P, 8, w]), op0=ALU.mult,
                                         op1=ALU.subtract).then_inc(pe_ok, 1)
                dve.tensor_tensor(es, sinks, mx, ALU.subtract).then_inc(esd_ok, 1)
                dve.wait_ge(exp_ok, n + 1)
                if first:
                    dve.memset(PR[:, :, 0:C], 0.0)
                dve.tensor_reduce(den, prk, AX_X, ALU.add).then_inc(den_ok, 1)
                dve.wait_ge(es_ok, n + 1)
                dve.wait_ge(den_ok, n * 2 + 1)
                dve.tensor_tensor(den, den, es, ALU.add).then_inc(den_ok, 1)
                dve.wait_ge(den_ok, n * 2 + 2)
                dve.reciprocal(den, den).then_inc(rden_ok, 1)
                for k in range(2):
                    if k:
                        dve.wait_ge(pt_mm, n + 1)
                        dve.tensor_copy(PT, heads(4)).then_inc(pt_ok, 1)
                        if last:
                            split_lo(T_DELTA, yd, 0, 6)
                    dve.wait_ge(blk_mm, s * WS + (B_GATE + 2 * c + k + 1))
                    dve.tensor_scalar(gates[:, bass.ds(s * WS + (2 * c + k), 1), :].rearrange("p a n -> p (a n)"),
                                      ps[:, k, :], par[:, bass.ds(s * WS + (PR_GATE + 2 * c + k), 1)], None,
                                      ALU.add).then_inc(blk_read, 1)

            dve.wait_ge(sink_ok, 2)
            attend(0, 0, 0, first=True)
            attend(1, 1, 0)
            with dve.Fori(1, S // P - 1) as s:
                for c in range(2):
                    attend(s * 2 + c, c, s)
            attend(6, 0, 3)
            attend(7, 1, 3, last=True)

            split_lo(T_DELTA, yd, 6, KT)
            dve.wait_ge(sig_ok, 1)
            for k in range(N_BR):
                if k == N_BR - 1:
                    split_lo(T_ATT, yatt, 0, KT - 1)
                dve.wait_ge(blk_mm, B_BRD + k + 1)
                dve.tensor_tensor(gates[:, 8 + k, :], gates[:, 8 + k, :], ps[:, k % 2, :], ALU.mult).then_inc(blk_read, 1)
            split_lo(T_ATT, yatt, KT - 1, KT)
            dve.wait_ge(sig_ok, 2)
            for k in range(N_BR):
                if k == N_BR - 1:
                    split_lo(T_MERGED, gates, 0, KT - 1)
                dve.wait_ge(blk_mm, B_BRA + k + 1)
                dve.tensor_tensor(gates[:, k, :], gates[:, k, :], ps[:, k % 2, :], ALU.mult).then_inc(blk_read, 1)
                dve.wait_ge(blk_read, B_BRA + k + 1)
                dve.tensor_tensor(gates[:, k, :], gates[:, k, :], gates[:, 8 + k, :], ALU.add).then_inc(mg_ok, 1)
            split_lo(T_MERGED, gates, KT - 1, KT)
            half = [slice(512 * n, 512 * n + 512) for n in range(2)]

            def residual(p, end, weigh):
                for t in range(TT):
                    dve.wait_ge(rows_mm, p * TT + t + 1)
                    cols, banks = (slice(0, D), ps[:, 2 * t:2 * t + 2, :]) if t < TT - 1 else (half[0], ps[:, 6:7, :])
                    dve.tensor_tensor(x1[:, t, cols], x1[:, t, cols], banks.rearrange("p b n -> p (b n)"),
                                      ALU.add).then_inc(x1_ok, 1)
                    if t > 0:
                        dve.wait_ge(rstd_ok, TT + p * TT + t)
                        weigh(t - 1)
                dve.wait_ge(blk_mm, end)
                dve.tensor_tensor(x1[:, TT - 1, half[1]], x1[:, TT - 1, half[1]], ps[:, 7, :], ALU.add).then_inc(x1_ok, 1)
                dve.wait_ge(ss_ok, TT + p * (TT + 1) + TT)
                dve.tensor_scalar(ms_half, ms_half, 1.0 / D, EPS, ALU.mult, ALU.add).then_inc(ms_ok, 1)
                dve.wait_ge(rstd_ok, TT + p * TT + TT)
                weigh(TT - 1)

            def scale_rows(t):
                dve.tensor_scalar(xn[:, t, :], x1[:, t, :], rstd[:, t:t + 1], None, ALU.mult).then_inc(xn_ok, 1)

            def finish(t):
                for cols in (slice(0, D),) if t < TT - 1 else half:
                    dve.scalar_tensor_tensor(out=x1[:, t, cols], in0=x1[:, t, cols], scalar=rstd[:, t:t + 1],
                                             in1=fw[:, cols], op0=ALU.mult, op1=ALU.mult).then_inc(y_fin, 1)

            dve.wait_ge(x_again, 16)
            residual(0, B_UP, scale_rows)
            norm_lo(T_MLP, PR_MLP)
            def square(k, i):
                dve.wait_ge(relu_ok, i * WS + (k + 1))
                a = a_t[:, bass.ds(i * WS + k, 1), :].rearrange("p a n -> p (a n)")
                dve.tensor_tensor(a, a, ps[:, k % 2, :], ALU.mult).then_inc(blk_read, 1)

            def squares_lo(i):
                for k in range(WS):
                    dve.wait_ge(a_hi_ok, i * WS + (T_SQ + k + 1))
                    dve.tensor_tensor(act_lo[:, k, :], a_t[:, bass.ds(i * WS + k, 1), :].rearrange("p a n -> p (a n)"),
                                      act_hi[:, k, :].bitcast(F32), ALU.subtract).then_inc(a_ok, 1)

            with dve.Fori(0, N_UP // WS - 1) as i:
                for k in range(WS):
                    square(k, i)
            for k in range(WS):
                if k == WS - 1:
                    squares_lo(0)
                square(k, N_UP // WS - 1)
            with dve.Fori(1, N_DOWN // WS) as i:
                squares_lo(i)
            dve.wait_ge(fw_ok, 16)
            residual(1, B_END, finish)


INPUTS = ["x", "norm_mix_w", "w_in", "b_gate", "attn_sinks", "conv_w", "a_log", "dt_bias", "dn_norm_w",
          "w_branch_attn", "w_branch_delta", "w_out", "norm_mlp_w", "w_mlp_up", "w_mlp_down", "final_norm_w"]


def shape_constants(np):
    i, j = np.arange(P)[:, None], np.arange(P)[None, :]
    same = i // C == j // C
    level = {b: (i // (2 * b) == j // (2 * b)) & (i % (2 * b) >= b) & (j % (2 * b) < b) for b in (1, 2, 4, 8, 16, 32)}
    mats = {"ident": i == j, "ones": np.ones((P, P)), "tri": same & (i <= j), "later": same & (i > j),
            "mask_t": np.where(same & (j >= i), 0.0, NEG), "mask_l": np.where(same & (i > j), 0.0, NEG),
            "m1": level[1], **{f"m{b}": level[b].T for b in (2, 4, 8, 16, 32)}}
    return np.ascontiguousarray(np.stack([mats[n] for n in CONSTS], axis=1).astype(np.float32))


def kernel(**inputs):
    import numpy as np
    import concourse.bacc as bacc
    from concourse.bass_utils import run_bass_kernel_spmd

    nc = bacc.Bacc("TRN2", target_bir_lowering=False, num_devices=1)
    arrays = {f"in_{n}": np.ascontiguousarray(inputs[n]) for n in INPUTS}
    arrays["in_shape_consts"] = shape_constants(np)
    args = [nc.dram_tensor(n, a.shape, mybir.dt.from_np(a.dtype), kind="ExternalInput").ap() for n, a in arrays.items()]
    args.append(nc.dram_tensor("out_0", (1, S, D), F32, kind="ExternalOutput").ap())
    build(nc, *args)
    return run_bass_kernel_spmd(nc, [arrays], core_ids=[0]).results[0]["out_0"]
```
